# Optimizing a Trainium2 kernel written in Bass

```python
import math
import jax
import jax.numpy as jnp
from jax import lax
import numpy as np
import jax, jax.numpy as jnp

D_MODEL = 1024
BATCH = 1
SEQ = 256
DEPTH = 1

HEAD_DIM = 64
ROPE_THETA = 10000.0
NORM_EPS = 1e-6
NEG_INF = -1e30
FORCE_SCORE = 1e9

DIFF_HEADS = 4
DIFF_VDIM = 2 * HEAD_DIM
DIFF_Q_BLOCK = 128

NSA_HEADS = 8
NSA_KV_GROUPS = 2
NSA_HPG = NSA_HEADS // NSA_KV_GROUPS
CMP_LEN = 32
CMP_STRIDE = 16
CMP_HIDDEN = 4 * HEAD_DIM
SEL_LEN = 64
SEL_TOPK = 16
WINDOW = 512
NSA_Q_BLOCK = 64

D_FF = int(math.ceil(8 * D_MODEL / 3 / 256)) * 256

DIFF_QK = DIFF_HEADS * 2 * HEAD_DIM
DIFF_V = DIFF_HEADS * DIFF_VDIM
NSA_Q = NSA_HEADS * HEAD_DIM
NSA_KV = NSA_KV_GROUPS * HEAD_DIM
NSA_GATES = 3 * NSA_HEADS
MERGE_GATES = 2 * D_MODEL
IN_SPLITS = (DIFF_QK, DIFF_QK, DIFF_V, NSA_Q, NSA_KV, NSA_KV, NSA_KV, NSA_KV, NSA_KV, NSA_KV, NSA_GATES, MERGE_GATES)
IN_DIM = sum(IN_SPLITS)
A_WIDTH = DIFF_V
B_WIDTH = NSA_HEADS * HEAD_DIM


def lambda_init(layer):
    return 0.8 - 0.6 * math.exp(-0.3 * layer)

def rms_norm(x, g):
    xf = x.astype(jnp.float32)
    y = xf * lax.rsqrt(jnp.mean(xf * xf, axis=-1, keepdims=True) + NORM_EPS)
    return (y * g.astype(jnp.float32)).astype(x.dtype)

def rope_tables(positions, dim):
    inv_freq = 1.0 / (ROPE_THETA ** (jnp.arange(0, dim, 2, dtype=jnp.float32) / dim))
    ang = positions.astype(jnp.float32)[..., None] * inv_freq
    return jnp.cos(ang), jnp.sin(ang)

def apply_rope(x, cos, sin):
    half = x.shape[-1] // 2
    xf = x.astype(jnp.float32)
    x1, x2 = xf[..., :half], xf[..., half:]
    return jnp.concatenate([x1 * cos - x2 * sin, x2 * cos + x1 * sin], axis=-1).astype(x.dtype)

def differential_attention(q, k, v, lam):
    B, S, H, _, dh = q.shape
    nblk = S // DIFF_Q_BLOCK
    scale = dh ** -0.5
    kpos = jnp.arange(S)

    def one_block(i):
        s0 = i * DIFF_Q_BLOCK
        qb = lax.dynamic_slice_in_dim(q, s0, DIFF_Q_BLOCK, axis=1)
        s = jnp.einsum('bqhcd,bkhcd->bhcqk', qb, k).astype(jnp.float32) * scale
        qpos = s0 + jnp.arange(DIFF_Q_BLOCK)
        causal = kpos[None, :] <= qpos[:, None]
        p = jax.nn.softmax(jnp.where(causal, s, NEG_INF), axis=-1)
        a = p[:, :, 0] - lam * p[:, :, 1]
        return jnp.einsum('bhqk,bkhe->bqhe', a.astype(v.dtype), v)

    o = lax.map(one_block, jnp.arange(nblk))
    return o.transpose(1, 0, 2, 3, 4).reshape(B, S, H, v.shape[-1])

def compress(x, pe, w1, w2):
    B, S, G, dh = x.shape
    nc = (S - CMP_LEN) // CMP_STRIDE + 1
    idx = np.arange(nc)[:, None] * CMP_STRIDE + np.arange(CMP_LEN)[None, :]
    blk = x[:, idx] + pe[None, None, :, None, :]
    blk = blk.transpose(0, 1, 3, 2, 4).reshape(B, nc, G, CMP_LEN * dh)
    return jax.nn.silu(blk @ w1) @ w2

def nsa_attention(q, kc, vc, ks, vs, kw, vw):
    B, S, G, hpg, dh = q.shape
    nc = kc.shape[1]
    nsb = S // SEL_LEN
    topk = min(SEL_TOPK, nsb)
    nblk = S // NSA_Q_BLOCK
    scale = dh ** -0.5
    cmp_end = np.arange(nc) * CMP_STRIDE + CMP_LEN - 1
    ci = np.arange(nc)[:, None] * CMP_STRIDE
    sj = np.arange(nsb)[None, :] * SEL_LEN
    overlap = jnp.asarray(((ci < sj + SEL_LEN) & (ci + CMP_LEN > sj)).astype(np.float32))
    kb = ks.reshape(B, nsb, SEL_LEN, G, dh).transpose(0, 3, 1, 2, 4)
    vb = vs.reshape(B, nsb, SEL_LEN, G, dh).transpose(0, 3, 1, 2, 4)
    kw_pad = jnp.pad(kw, ((0, 0), (WINDOW, 0), (0, 0), (0, 0)))
    vw_pad = jnp.pad(vw, ((0, 0), (WINDOW, 0), (0, 0), (0, 0)))
    b_idx = jnp.arange(B)[:, None, None, None]
    g_idx = jnp.arange(G)[None, None, :, None]
    blk_ids = jnp.arange(nsb)
    sel_off = jnp.arange(SEL_LEN)

    def one_block(i):
        s0 = i * NSA_Q_BLOCK
        qpos = s0 + jnp.arange(NSA_Q_BLOCK)
        qb = lax.dynamic_slice_in_dim(q, s0, NSA_Q_BLOCK, axis=1)
        sc = jnp.einsum('bqghd,bcgd->bqghc', qb, kc).astype(jnp.float32) * scale
        cm = (cmp_end[None, :] <= qpos[:, None])[None, :, None, None, :]
        pc = jax.nn.softmax(jnp.where(cm, sc, NEG_INF), axis=-1) * cm
        o_c = jnp.einsum('bqghc,bcgd->bqghd', pc.astype(vc.dtype), vc)
        imp = jnp.einsum('bqgc,cn->bqgn', pc.sum(axis=3), overlap)
        qblk = qpos // SEL_LEN
        forced = (blk_ids[None, :] == 0) | (blk_ids[None, :] == qblk[:, None]) | (blk_ids[None, :] == qblk[:, None] - 1)
        causal_blk = blk_ids[None, :] <= qblk[:, None]
        imp = jnp.where(forced[None, :, None, :], FORCE_SCORE, imp)
        imp = jnp.where(causal_blk[None, :, None, :], imp, NEG_INF)
        _, idx = lax.top_k(imp, topk)
        ksel = kb[b_idx, g_idx, idx]
        vsel = vb[b_idx, g_idx, idx]
        ss = jnp.einsum('bqghd,bqgnld->bqghnl', qb, ksel).astype(jnp.float32) * scale
        kp = idx[..., None] * SEL_LEN + sel_off
        smask = (kp <= qpos[None, :, None, None, None])[:, :, :, None]
        ss = jnp.where(smask, ss, NEG_INF).reshape(B, NSA_Q_BLOCK, G, hpg, topk * SEL_LEN)
        ps = jax.nn.softmax(ss, axis=-1).reshape(B, NSA_Q_BLOCK, G, hpg, topk, SEL_LEN)
        o_s = jnp.einsum('bqghnl,bqgnld->bqghd', ps.astype(vsel.dtype), vsel)
        kwb = lax.dynamic_slice_in_dim(kw_pad, s0, NSA_Q_BLOCK + WINDOW, axis=1)
        vwb = lax.dynamic_slice_in_dim(vw_pad, s0, NSA_Q_BLOCK + WINDOW, axis=1)
        kpos = s0 - WINDOW + jnp.arange(NSA_Q_BLOCK + WINDOW)
        dist = qpos[:, None] - kpos[None, :]
        wmask = ((dist >= 0) & (dist < WINDOW) & (kpos[None, :] >= 0))[None, :, None, None, :]
        sw = jnp.einsum('bqghd,bkgd->bqghk', qb, kwb).astype(jnp.float32) * scale
        pw = jax.nn.softmax(jnp.where(wmask, sw, NEG_INF), axis=-1)
        o_w = jnp.einsum('bqghk,bkgd->bqghd', pw.astype(vwb.dtype), vwb)
        return o_c, o_s, o_w

    o_c, o_s, o_w = lax.map(one_block, jnp.arange(nblk))

    def to_seq(o):
        return o.transpose(1, 0, 2, 3, 4, 5).reshape(B, S, G * hpg, dh)

    return to_seq(o_c), to_seq(o_s), to_seq(o_w)

def hybrid_mixer(u, cos, sin, layer, w_in, diff_lambda, diff_subln_g, cmp_pe_k, cmp_pe_v,
                 cmp_k_w1, cmp_k_w2, cmp_v_w1, cmp_v_w2, w_branch_a, w_branch_b, w_out):
    B, S, _ = u.shape
    G, dh = NSA_KV_GROUPS, HEAD_DIM
    split_at = np.cumsum(IN_SPLITS)[:-1].tolist()
    (dq, dk, dv, nq, kc_, vc_, ks_, vs_, kw_, vw_, ngate, mgate) = jnp.split(u @ w_in, split_at, axis=-1)
    c4, s4 = cos[:, :, None, None, :], sin[:, :, None, None, :]
    c3, s3 = cos[:, :, None, :], sin[:, :, None, :]
    dq = apply_rope(dq.reshape(B, S, DIFF_HEADS, 2, dh), c4, s4)
    dk = apply_rope(dk.reshape(B, S, DIFF_HEADS, 2, dh), c4, s4)
    dv = dv.reshape(B, S, DIFF_HEADS, DIFF_VDIM)
    lam_init = lambda_init(layer)
    lf = diff_lambda.astype(jnp.float32)
    lam = jnp.exp(jnp.sum(lf[0] * lf[1])) - jnp.exp(jnp.sum(lf[2] * lf[3])) + lam_init
    y_a = differential_attention(dq, dk, dv, lam)
    y_a = rms_norm(y_a, diff_subln_g) * (1.0 - lam_init)
    y_a = y_a.reshape(B, S, A_WIDTH) @ w_branch_a
    nq = apply_rope(nq.reshape(B, S, NSA_HEADS, dh), c3, s3).reshape(B, S, G, NSA_HPG, dh)

    def kv(t):
        return t.reshape(B, S, G, dh)

    k_cmp = compress(apply_rope(kv(kc_), c3, s3), cmp_pe_k, cmp_k_w1, cmp_k_w2)
    v_cmp = compress(kv(vc_), cmp_pe_v, cmp_v_w1, cmp_v_w2)
    k_sel = apply_rope(kv(ks_), c3, s3)
    k_win = apply_rope(kv(kw_), c3, s3)
    o_c, o_s, o_w = nsa_attention(nq, k_cmp, v_cmp, k_sel, kv(vs_), k_win, kv(vw_))
    g = jax.nn.sigmoid(ngate.astype(jnp.float32)).reshape(B, S, 3, NSA_HEADS, 1).astype(u.dtype)
    y_b = g[:, :, 0] * o_c + g[:, :, 1] * o_s + g[:, :, 2] * o_w
    y_b = y_b.reshape(B, S, B_WIDTH) @ w_branch_b
    mg = jax.nn.sigmoid(mgate.astype(jnp.float32)).reshape(B, S, 2, D_MODEL).astype(u.dtype)
    return (mg[:, :, 0] * y_a + mg[:, :, 1] * y_b) @ w_out

def swiglu(u, w_gate, w_up, w_down):
    return (jax.nn.silu(u @ w_gate) * (u @ w_up)) @ w_down

def first_inputs(seed: int = 0) -> dict:
    key = jax.random.key(seed)
    ks = jax.random.split(key, 22)

    def nrm(k, shape, scale):
        return jax.random.normal(k, shape, jnp.float32) * scale

    return {
        "x": nrm(ks[0], (BATCH, SEQ, D_MODEL), 1.0),
        "positions": jnp.tile(jnp.arange(SEQ, dtype=jnp.int32)[None, :], (BATCH, 1)),
        "attn_norm_g": 1.0 + nrm(ks[1], (DEPTH, D_MODEL), 0.02),
        "w_in": nrm(ks[2], (DEPTH, D_MODEL, IN_DIM), D_MODEL ** -0.5),
        "diff_lambda": nrm(ks[3], (DEPTH, 4, HEAD_DIM), 0.1),
        "diff_subln_g": 1.0 + nrm(ks[4], (DEPTH, DIFF_VDIM), 0.02),
        "cmp_pe_k": nrm(ks[5], (DEPTH, CMP_LEN, HEAD_DIM), 0.1),
        "cmp_pe_v": nrm(ks[6], (DEPTH, CMP_LEN, HEAD_DIM), 0.1),
        "cmp_k_w1": nrm(ks[7], (DEPTH, CMP_LEN * HEAD_DIM, CMP_HIDDEN), (CMP_LEN * HEAD_DIM) ** -0.5),
        "cmp_k_w2": nrm(ks[8], (DEPTH, CMP_HIDDEN, HEAD_DIM), CMP_HIDDEN ** -0.5),
        "cmp_v_w1": nrm(ks[9], (DEPTH, CMP_LEN * HEAD_DIM, CMP_HIDDEN), (CMP_LEN * HEAD_DIM) ** -0.5),
        "cmp_v_w2": nrm(ks[10], (DEPTH, CMP_HIDDEN, HEAD_DIM), CMP_HIDDEN ** -0.5),
        "w_branch_a": nrm(ks[11], (DEPTH, A_WIDTH, D_MODEL), A_WIDTH ** -0.5),
        "w_branch_b": nrm(ks[12], (DEPTH, B_WIDTH, D_MODEL), B_WIDTH ** -0.5),
        "w_out": nrm(ks[13], (DEPTH, D_MODEL, D_MODEL), D_MODEL ** -0.5),
        "ffn_norm_g": 1.0 + nrm(ks[14], (DEPTH, D_MODEL), 0.02),
        "w_gate": nrm(ks[15], (DEPTH, D_MODEL, D_FF), D_MODEL ** -0.5),
        "w_up": nrm(ks[16], (DEPTH, D_MODEL, D_FF), D_MODEL ** -0.5),
        "w_down": nrm(ks[17], (DEPTH, D_FF, D_MODEL), D_FF ** -0.5),
        "final_norm_g": 1.0 + nrm(ks[18], (D_MODEL,), 0.02),
    }

def first_block(x, positions, attn_norm_g, w_in, diff_lambda, diff_subln_g, cmp_pe_k, cmp_pe_v,
              cmp_k_w1, cmp_k_w2, cmp_v_w1, cmp_v_w2, w_branch_a, w_branch_b, w_out,
              ffn_norm_g, w_gate, w_up, w_down, final_norm_g):
    cos, sin = rope_tables(positions, HEAD_DIM)
    h = x
    for layer in range(DEPTH):
        u = rms_norm(h, attn_norm_g[layer])
        h = h + hybrid_mixer(u, cos, sin, layer, w_in[layer], diff_lambda[layer], diff_subln_g[layer],
                             cmp_pe_k[layer], cmp_pe_v[layer], cmp_k_w1[layer], cmp_k_w2[layer],
                             cmp_v_w1[layer], cmp_v_w2[layer], w_branch_a[layer], w_branch_b[layer],
                             w_out[layer])
        u = rms_norm(h, ffn_norm_g[layer])
        h = h + swiglu(u, w_gate[layer], w_up[layer], w_down[layer])
    return rms_norm(h, final_norm_g)


GRID_W = 64
ATTN_HEADS = 8
ATTN_WIDTH = ATTN_HEADS * HEAD_DIM
WIN_ROWS = 8
WIN_COLS = 16
Q_COLS = 16
BAND_COLS = 2 * WIN_COLS
CONV_WIDTH = D_MODEL - ATTN_WIDTH
CONV_K = 31
IN_WIDTH = 3 * ATTN_WIDTH + 2 * CONV_WIDTH
N_EXPERTS = 16
EC_CAPACITY_FACTOR = 2
EXPERT_FF = 2048


def rms_norm_2(x, g):
    x32 = x.astype(jnp.float32)
    y = x32 * lax.rsqrt(jnp.mean(x32 * x32, axis=-1, keepdims=True) + NORM_EPS)
    return (y * g.astype(jnp.float32)).astype(x.dtype)

def layer_norm(x, g, b):
    x32 = x.astype(jnp.float32)
    mu = jnp.mean(x32, axis=-1, keepdims=True)
    var = jnp.mean(jnp.square(x32 - mu), axis=-1, keepdims=True)
    y = (x32 - mu) * lax.rsqrt(var + NORM_EPS)
    return (y * g.astype(jnp.float32) + b.astype(jnp.float32)).astype(x.dtype)

def neighbourhood_attention(q, k, v, rpb):
    B, S, H, Dh = q.shape
    rows = S // GRID_W
    kh = min(WIN_ROWS, rows)
    n_cb = GRID_W // Q_COLS
    r = jnp.arange(rows)
    row_start = jnp.clip(r - kh // 2, 0, rows - kh)
    row_idx = row_start[:, None] + jnp.arange(kh)[None, :]
    cb = jnp.arange(n_cb)
    band_start = jnp.clip(cb * Q_COLS - WIN_COLS // 2, 0, GRID_W - BAND_COLS)
    col_idx = band_start[:, None] + jnp.arange(BAND_COLS)[None, :]
    qc = cb[:, None] * Q_COLS + jnp.arange(Q_COLS)[None, :]
    win_start = jnp.clip(qc - WIN_COLS // 2, 0, GRID_W - WIN_COLS)
    kc = col_idx[:, None, :]
    col_mask = (kc >= win_start[..., None]) & (kc < win_start[..., None] + WIN_COLS)
    row_off = row_idx - r[:, None] + (WIN_ROWS - 1)
    col_off = jnp.clip(kc - qc[..., None] + (WIN_COLS - 1), 0, 2 * WIN_COLS - 2)
    bias = rpb[:, row_off[:, None, None, :, None], col_off[None, :, :, None, :]]
    qg = q.reshape(B, rows, n_cb, Q_COLS, H, Dh)
    kgrid = k.reshape(B, rows, GRID_W, H, Dh)
    vgrid = v.reshape(B, rows, GRID_W, H, Dh)
    ri = row_idx[:, None, :, None]
    ci = col_idx[None, :, None, :]
    kg = kgrid[:, ri, ci]
    vg = vgrid[:, ri, ci]
    s = jnp.einsum('brcqhd,brckwhd->bhrcqkw', qg, kg,
                   preferred_element_type=jnp.float32) * (Dh ** -0.5)
    s = s + bias.astype(jnp.float32)[None]
    s = jnp.where(col_mask[:, :, None, :], s, -jnp.inf)
    p = jax.nn.softmax(s, axis=(-2, -1))
    o = jnp.einsum('bhrcqkw,brckwhd->brcqhd', p.astype(v.dtype), vg)
    return o.reshape(B, S, H * Dh)

def conformer_conv(a, gate, conv_w, conv_b, ln_g, ln_b):
    C = a.shape[-1]
    u = a * jax.nn.sigmoid(gate)
    dw = lax.conv_general_dilated(
        u, conv_w[:, None, :].astype(u.dtype), window_strides=(1,),
        padding=[(CONV_K // 2, CONV_K // 2)],
        dimension_numbers=('NWC', 'WIO', 'NWC'), feature_group_count=C)
    dw = dw + conv_b
    return jax.nn.silu(layer_norm(dw, ln_g, ln_b))

def expert_choice_ffn(h, w_router, w_gate, w_up, w_down):
    B, S, D = h.shape
    cap = EC_CAPACITY_FACTOR * S // N_EXPERTS
    logits = jnp.einsum('bsd,de->bse', h, w_router, preferred_element_type=jnp.float32)
    aff = jax.nn.softmax(logits, axis=-1)
    gates, idx = lax.top_k(jnp.swapaxes(aff, 1, 2), cap)
    bidx = jnp.arange(B)[:, None, None]
    xs = h[bidx, idx]
    hid = jax.nn.silu(jnp.einsum('becd,edf->becf', xs, w_gate)) * jnp.einsum('becd,edf->becf', xs, w_up)
    eo = jnp.einsum('becf,efd->becd', hid, w_down)
    return jnp.zeros_like(h).at[bidx, idx].add(gates[..., None].astype(h.dtype) * eo)

def second_inputs(seed: int = 0) -> dict:
    key = jax.random.key(seed)
    ks = jax.random.split(key, 20)
    f32 = jnp.float32
    nrm = lambda k, shape, scale: jax.random.normal(k, shape, f32) * scale
    gain = lambda k, shape: 1.0 + 0.02 * jax.random.normal(k, shape, f32)
    return {
        "x": jax.random.normal(ks[0], (BATCH, SEQ, D_MODEL), f32),
        "norm1_g": gain(ks[1], (DEPTH, D_MODEL)),
        "w_in": nrm(ks[2], (DEPTH, D_MODEL, IN_WIDTH), D_MODEL ** -0.5),
        "rpb": nrm(ks[3], (DEPTH, ATTN_HEADS, 2 * WIN_ROWS - 1, 2 * WIN_COLS - 1), 0.02),
        "conv_w": nrm(ks[4], (DEPTH, CONV_K, CONV_WIDTH), CONV_K ** -0.5),
        "conv_b": nrm(ks[5], (DEPTH, CONV_WIDTH), 0.02),
        "conv_ln_g": gain(ks[6], (DEPTH, CONV_WIDTH)),
        "conv_ln_b": nrm(ks[7], (DEPTH, CONV_WIDTH), 0.02),
        "attn_out_g": gain(ks[8], (DEPTH, ATTN_WIDTH)),
        "conv_out_g": gain(ks[9], (DEPTH, CONV_WIDTH)),
        "w_out": nrm(ks[10], (DEPTH, D_MODEL, D_MODEL), (2 * DEPTH * D_MODEL) ** -0.5),
        "norm2_g": gain(ks[11], (DEPTH, D_MODEL)),
        "w_router": nrm(ks[12], (DEPTH, D_MODEL, N_EXPERTS), D_MODEL ** -0.5),
        "w_gate": nrm(ks[13], (DEPTH, N_EXPERTS, D_MODEL, EXPERT_FF), D_MODEL ** -0.5),
        "w_up": nrm(ks[14], (DEPTH, N_EXPERTS, D_MODEL, EXPERT_FF), D_MODEL ** -0.5),
        "w_down": nrm(ks[15], (DEPTH, N_EXPERTS, EXPERT_FF, D_MODEL), (2 * DEPTH * EXPERT_FF) ** -0.5),
        "final_g": gain(ks[16], (D_MODEL,)),
    }

def second_block(x, norm1_g, w_in, rpb, conv_w, conv_b, conv_ln_g, conv_ln_b,
              attn_out_g, conv_out_g, w_out, norm2_g, w_router, w_gate, w_up,
              w_down, final_g):
    B, S, _ = x.shape
    splits = [ATTN_WIDTH, 2 * ATTN_WIDTH, 3 * ATTN_WIDTH, 3 * ATTN_WIDTH + CONV_WIDTH]
    for l in range(DEPTH):
        h = rms_norm_2(x, norm1_g[l])
        proj = jnp.einsum('bsd,de->bse', h, w_in[l])
        q, k, v, a, g = jnp.split(proj, splits, axis=-1)
        q = q.reshape(B, S, ATTN_HEADS, HEAD_DIM)
        k = k.reshape(B, S, ATTN_HEADS, HEAD_DIM)
        v = v.reshape(B, S, ATTN_HEADS, HEAD_DIM)
        attn = neighbourhood_attention(q, k, v, rpb[l])
        conv = conformer_conv(a, g, conv_w[l], conv_b[l], conv_ln_g[l], conv_ln_b[l])
        mixed = jnp.concatenate([rms_norm_2(attn, attn_out_g[l]), rms_norm_2(conv, conv_out_g[l])], axis=-1)
        x = x + jnp.einsum('bse,ed->bsd', mixed, w_out[l])
        h = rms_norm_2(x, norm2_g[l])
        x = x + expert_choice_ffn(h, w_router[l], w_gate[l], w_up[l], w_down[l])
    return rms_norm_2(x, final_g)


def setup_inputs(seed=0):
    out = dict(first_inputs(seed))
    for name, value in second_inputs(seed + 1).items():
        if name != "x":
            out[name + "_2"] = value
    return out


def reference(
    x, positions, attn_norm_g, w_in, diff_lambda, diff_subln_g, cmp_pe_k, cmp_pe_v, cmp_k_w1,
    cmp_k_w2, cmp_v_w1, cmp_v_w2, w_branch_a, w_branch_b, w_out, ffn_norm_g, w_gate, w_up,
    w_down, final_norm_g, norm1_g_2, w_in_2, rpb_2, conv_w_2, conv_b_2, conv_ln_g_2,
    conv_ln_b_2, attn_out_g_2, conv_out_g_2, w_out_2, norm2_g_2, w_router_2, w_gate_2, w_up_2,
    w_down_2, final_g_2,
):
    x = first_block(
        x, positions, attn_norm_g, w_in, diff_lambda, diff_subln_g, cmp_pe_k, cmp_pe_v,
        cmp_k_w1, cmp_k_w2, cmp_v_w1, cmp_v_w2, w_branch_a, w_branch_b, w_out, ffn_norm_g,
        w_gate, w_up, w_down, final_norm_g,
    )
    return second_block(
        x, norm1_g_2, w_in_2, rpb_2, conv_w_2, conv_b_2, conv_ln_g_2, conv_ln_b_2, attn_out_g_2,
        conv_out_g_2, w_out_2, norm2_g_2, w_router_2, w_gate_2, w_up_2, w_down_2, final_g_2,
    )


_drawn_inputs = setup_inputs


def setup_inputs(seed=0):
    import zlib

    import numpy as np

    out = dict(_drawn_inputs(seed))
    spreads = {}
    factors = {'attn_norm_g': 2.722,
     'diff_lambda': 8.0,
     'diff_subln_g': 4.414,
     'cmp_pe_k': 8.0,
     'ffn_norm_g': 3.424,
     'norm1_g_2': 3.272,
     'rpb_2': 8.0,
     'conv_b_2': 3.448,
     'conv_ln_g_2': 4.541,
     'conv_ln_b_2': 6.15,
     'attn_out_g_2': 6.009,
     'conv_out_g_2': 6.209,
     'norm2_g_2': 6.327,
     'final_g_2': 2.713}
    for name, (base, spread) in spreads.items():
        noise = np.random.default_rng([zlib.crc32(name.encode()), seed]).standard_normal(out[name].shape)
        drawn = base * np.exp(spread * noise) if base else spread * noise
        out[name] = jnp.asarray(drawn.astype(out[name].dtype))
    for name, factor in factors.items():
        out[name] = (out[name] * factor).astype(out[name].dtype)
    return out
```

```python
import math
from contextlib import ExitStack

import numpy as np

import concourse.bass as bass
from concourse import mybir

ALU = mybir.AluOpType
ACT = mybir.ActivationFunctionType
AX_X = mybir.AxisListType.X
F32 = mybir.dt.float32
I32 = mybir.dt.int32
U32 = mybir.dt.uint32

P = 128
S = 256
T = S // P
D = 1024
KD = D // P
DH = 64
HALF = DH // 2
NB = 512
BANKS = 8
EPS = 1e-6
NEG = -1e30
SCALE = DH ** -0.5
THETA = 10000.0
LAM_INIT = 0.8 - 0.6 * math.exp(0.0)

W_IN_CUTS = [(0, 512), (512, 512), (1024, 512), (1536, 512), (2048, 512), (2560, 280),
             (2840, 512), (3352, 512), (3864, 512), (4376, 512)]
DQ, DK, DV, NQ, KV4, KV2 = range(6)
MG0 = 6
CMP_LEN, CMP_STRIDE = 32, 16
NCB = (S - CMP_LEN) // CMP_STRIDE + 1
CH = 256
LP = CMP_LEN // 2
FF = 2816
GU = 256
FC = FF // GU
FK = FF // P

GRID = 64
ROWS = S // GRID
WIN_C = 16
RPB_R, RPB_C = 15, 31
NH2 = 8
CW = 512
CT = CW // P
TAPS = 31
PAD = TAPS // 2
E = 16
CAP = 2 * S // E
EF = 2048
FJ = EF // NB

SLOTS = 8
SLOT = 4096
XCH = 12

GAIN_ROWS = {}
_at = 0
for _name, _n in (("attn", 8), ("ffn", 8), ("norm1", 8), ("norm2", 8), ("attn_out", 4), ("conv_out", 4),
                  ("conv_b", 4), ("ln_g", 4), ("ln_b", 4), ("subln", 1), ("pe_k", 16), ("pe_v", 16)):
    GAIN_ROWS[_name] = (_at, _n)
    _at += _n
GAINS = _at

UNITS1 = ([("diff", p, t) for p in range(2) for t in range(T)] + [("cmp", 0, t) for t in range(T)]
          + [("sel", p, t) for p in range(2) for t in range(T)] + [("win", p, t) for p in range(2) for t in range(T)])
UNITS2 = [("grid", p, t) for p in range(2) for t in range(T)]
UNITS = UNITS1 + UNITS2
NU1 = len(UNITS1)


def key_tiles(u):
    kind, _, t = UNITS[u]
    return T if kind == "grid" else (1 if kind == "cmp" else t + 1)


def turns(u):
    kind = UNITS[u][0]
    if kind == "cmp":
        return 2
    if kind == "diff":
        return 1
    return key_tiles(u)


def order_of_steps():
    st = [("gains",), ("norm", 0)]
    lag = []
    for c in range(6):
        for t in range(T):
            st.append(("proj", c, t))
            if len(lag) > 1:
                st.append(("rot",) + lag.pop(0))
            if c != DV:
                lag.append((c, t))
    fill = {0: [("blocks",), ("proj", MG0, 0)], 1: [("cmph",), ("proj", MG0, 1)], 2: [("cmpt",), ("proj", MG0 + 1, 0)],
            3: [("cmpw",), ("proj", MG0 + 1, 1)], 4: [("proj", MG0 + 2, 0)], 5: [("proj", MG0 + 2, 1)],
            6: [("yan",), ("proj", MG0 + 3, 0)], 7: [("yas",), ("proj", MG0 + 3, 1)], 8: [("yaT",), ("mgs",)],
            10: [("bra", 0, 0)], 11: [("bra", 1, 0)], 12: [("bra", 0, 1)], 13: [("bra", 1, 1)]}
    st += [("rot",) + x for x in lag]
    for i in range(NU1 + 2):
        if i < NU1:
            st.append(("S", i))
        st += fill.get(i, [])
        if 1 <= i <= NU1:
            st.append(("PT", i - 1))
        if i >= 2:
            st.append(("PV", i - 2))
    st.append(("ybT",))
    st += [("brb", t, h) for h in range(2) for t in range(T)]
    st.append(("mT",))
    st += [("wo", t, h) for h in range(2) for t in range(T)]
    st.append(("norm", 1))
    for c in range(FC):
        st += [("gu", c, t) for t in range(T)]
        if c:
            st.append(("hT", c - 1))
    st += [("hT", FC - 1), ("down",), ("norm", 2)]
    st += [("qk", c, h) for c in range(2) for h in range(2)] + [("v", t) for t in range(T)]
    fill = {0: [("ag", 0, 0), ("ag", 0, 1)], 1: [("ag", 1, 0), ("ag", 1, 1)]}
    n2 = len(UNITS2)
    for i in range(n2 + 2):
        if i < n2:
            st.append(("S", NU1 + i))
        st += fill.get(i, [])
        if 1 <= i <= n2:
            st.append(("PT", NU1 + i - 1))
        if i >= 2:
            st.append(("PV", NU1 + i - 2))
    st += [("on",), ("oT",), ("conv",), ("cmean",), ("cvar",), ("crms",)]
    st += [("wo2", t, h) for h in range(2) for t in range(T)]
    st += [("norm", 3), ("logit",), ("affT",), ("spread",), ("cols",)]
    return st


def jobs_of(step):
    kind = step[0]
    n = {"gains": 2, "norm": 4, "yaT": T, "ybT": T, "mT": 4, "down": 4, "oT": T, "S": 2, "blocks": 0, "yan": 0, "yas": 0,
         "mgs": 0, "on": 0, "conv": 0}.get(kind, 1)
    if kind == "PT":
        n = turns(step[1])
    return [step + (i,) for i in range(n)]


def two_blocks(nc, A, out):
    STEPS = order_of_steps()
    JOB = {}
    for st in STEPS:
        for j in jobs_of(st):
            JOB[j] = len(JOB)

    CHUNKS = ([("w_in", c) for c in range(6)] + [("cmp", 0), ("cmp", 1)] + [("w_in", c) for c in range(MG0, 10)]
              + [("bra",), ("brb",), ("wo", 0), ("wo", 1)])
    SLOT_OF = {ch: i % 5 for i, ch in enumerate(CHUNKS)}
    late = ([("gu", c) for c in range(FC)] + [("down", i) for i in range(6)] + [("w_in2", c) for c in range(5)]
            + [("wo2", 0), ("wo2", 1)])
    SLOT_OF.update({ch: i % 7 for i, ch in enumerate(late)})
    CHUNKS += late
    LAST_USE = {("cmp", 0): ("cmph", 0), ("cmp", 1): ("cmph", 0), ("bra",): ("bra", 1, 1, 0), ("brb",): ("brb", 1, 1, 0)}
    for c in range(10):
        LAST_USE[("w_in", c)] = ("proj", c, 1, 0)
    for h in range(2):
        LAST_USE[("wo", h)] = ("wo", 1, h, 0)
        LAST_USE[("wo2", h)] = ("wo2", 1, h, 0)
        LAST_USE[("w_in2", h)] = ("qk", h, 1, 0)
        LAST_USE[("w_in2", 3 + h)] = ("ag", h, 1, 0)
    LAST_USE[("w_in2", 2)] = ("v", 1, 0)
    for c in range(FC):
        LAST_USE[("gu", c)] = ("gu", c, 1, 0)
    LAST_USE[("down", 5)] = ("down", 3)

    with ExitStack() as ctx:
        def sb(name, *shape, dt=F32):
            return ctx.enter_context(nc.sbuf_tensor(name, list(shape), dt))

        def sem(name):
            return ctx.enter_context(nc.semaphore(name))

        bank = [ctx.enter_context(nc.psum_tensor(f"bank{b}", [P, NB], F32)) for b in range(BANKS)]

        ring = sb("ring", P, SLOTS, SLOT)
        ident = sb("ident", P, P)
        ones = sb("ones", P, P)
        causal = sb("causal", P, S)
        cmp_add = sb("cmp_add", P, T, 16)
        cmp_keep = sb("cmp_keep", P, T, 16)
        delta = sb("delta", E, E, CAP)
        tok_free = sb("tok_free", P, S)
        tok_int = sb("tok_int", P, S, dt=I32)
        part_int = sb("part_int", P, T, dt=I32)
        tok_part = sb("tok_part", P, T)
        inv_freq = sb("inv_freq", P, HALF)
        pos_int = sb("pos_int", P, T, dt=I32)
        pos = sb("pos", P, T)
        trig = sb("trig", P, 3, T, HALF)
        ang = sb("ang", P, T * HALF)
        angk = sb("angk", P, T * HALF)
        gain = sb("gain", P, 96)
        convw = sb("convw", P, TAPS, CT)
        subln = sb("subln", P, 1)
        ystat = sb("ystat", P, 16)
        mhalf = sb("mhalf", P, 8)
        eps_col = sb("eps_col", P, 1)
        w_r = sb("w_r", P, KD, E)
        w2 = sb("w2", P, 2, 2, DH)
        dl = sb("dl", P, 4, DH)
        dlp = sb("dlp", P, 2, DH)
        lamv = sb("lamv", P, 8)
        stat = sb("stat", P, 64)
        nmax = sb("nmax", P, len(UNITS), 8)
        rsum = sb("rsum", P, len(UNITS), 8)
        rinv = sb("rinv", P, len(UNITS), 8)
        kcT = sb("kcT", P, 16)
        vcs = sb("vcs", P, 2 * DH)
        rpbp = sb("rpbp", P, P)
        X = sb("X", P, T, D)
        UT = sb("UT", P, KD, S)
        SC = sb("SC", P, T, D)
        GB = sb("GB", P, D)
        ARENA = 9200
        arena = sb("arena", P, ARENA)

        def carve(base, sizes):
            views, at = [], 0
            for n in sizes:
                views.append(base[:, at:at + n])
                at += n
            assert at <= base.shape[1], (at, base.shape)
            return views

        vsel, vwin, ngate, hidc, hidcT, probs_, turned_, ya_, yb_, kswap = carve(
            arena, [T * P, T * P, T * 24, CH, 2 * DH, 2 * 1024, 2 * 1024, T * NB, T * NB, 2 * S])
        over = ring[:, 5:8, :].rearrange("p a b -> p (a b)")
        qkT, mg, yaT, ybT, vdiff, blk = carve(over, [16 * S, T * 2 * D, 4 * S, 4 * S, T * NB, 2 * LP * 32])
        qkT = qkT.rearrange("p (b s) -> p b s", s=S)
        mg = mg.rearrange("p (t c) -> p t c", t=T)
        yaT = yaT.rearrange("p (b s) -> p b s", s=S)
        ybT = ybT.rearrange("p (b s) -> p b s", s=S)
        vdiff = vdiff.rearrange("p (t c) -> p t c", t=T)
        blk = blk.rearrange("p (v l g i) -> p v l g i", v=2, l=LP, g=2)
        vsel = vsel.rearrange("p (t c) -> p t c", t=T)
        vwin = vwin.rearrange("p (t c) -> p t c", t=T)
        ngate = ngate.rearrange("p (t b h) -> p t b h", t=T, b=3)
        hidcT = hidcT.rearrange("p (k c) -> p k c", k=2)
        kswap = kswap.rearrange("p (v s) -> p v s", v=2)
        ya = ya_.rearrange("p (t c) -> p t c", t=T)
        yb = yb_.rearrange("p (t c) -> p t c", t=T)
        UTf = UT[:, :, :].rearrange("p k s -> p (k s)").rearrange("p (t d) -> p t d", t=T)
        scf = SC[:, :, :].rearrange("p t c -> p (t c)")
        rope_a, rope_b = scf[:, 0:NB], scf[:, NB:2 * NB]
        rot = scf[:, 2 * NB:4 * NB].rearrange("p (b c) -> p b c", b=2)
        sgate = scf[:, 0:2 * GU].rearrange("p (b c) -> p b c", b=2)
        hid = scf[:, 2 * GU:6 * GU].rearrange("p (b c) -> p b c", b=4)
        hidT = arena[:, 0:FK * S].rearrange("p (k s) -> p k s", s=S)
        probs2_, qkT2_, v2_ = carve(arena, [2 * 1024, 8 * S, T * NB])
        bias = arena[:, ARENA - 3072:ARENA].rearrange("p (h d c) -> p h d c", h=NH2, d=6)
        qkT2 = qkT2_.rearrange("p (b s) -> p b s", s=S)
        v2 = v2_.rearrange("p (t c) -> p t c", t=T)
        o2 = GB[:, :].rearrange("p (t c) -> p t c", t=T)
        upad_, dw_, cz_, sg2_ = carve(ring[:, 7, :], [CT * (S + 2 * PAD), CT * S, CT * S, 904])
        upad = upad_.rearrange("p (c s) -> p c s", c=CT)
        dw = dw_.rearrange("p (c s) -> p c s", c=CT)
        cz = cz_.rearrange("p (c s) -> p c s", c=CT)
        crs = sg2_[:, 0:S]
        probs1 = probs_.rearrange("p (b m k) -> p b m k", b=2, m=4)
        turned1 = turned_.rearrange("p (b n) -> p b n", b=2)
        probs2 = probs2_.rearrange("p (b m k) -> p b m k", b=2, m=4)
        turned2 = scf.rearrange("p (b n) -> p b n", b=2)
        (pick_, xsT_, sgx, hidx, hidxT_, eo_, spreadT_, routew, topv, topf, top4f, top4g, dgi, dgg, topi_, ecols_, affs_,
         aff_) = carve(arena, [T * E * CAP, KD * CAP, NB, NB, NB, 2 * NB, S, S, CAP, CAP, P, P, NB, 0, CAP, 2 * E, 64, 64])
        pick = pick_.rearrange("p (t n) -> p t n", t=T)
        xsT = xsT_.rearrange("p (k s) -> p k s", s=CAP)
        hidxT = hidxT_.rearrange("p (c n) -> p c n", c=4)
        eo = eo_.rearrange("p (h n) -> p h n", h=2)
        ecols = ecols_.rearrange("p (v e) -> p v e", v=2)
        aff = aff_[:, 0:T * E].rearrange("p (t e) -> p t e", t=T)
        topi = topi_.bitcast(U32)

        full = [sem(f"bank_full{b}") for b in range(BANKS)]
        free = [sem(f"bank_free{b}") for b in range(BANKS)]
        loaded = [sem(f"slot_loaded{s}") for s in range(SLOTS)]
        used = [sem(f"slot_used{s}") for s in range(SLOTS)]
        down_used = sem("down_chunk_used")
        x_loaded, rows_loaded, conv_loaded = sem("x_loaded"), sem("rows_loaded"), sem("conv_loaded")
        small_loaded, gb_loaded, gb2_loaded = sem("small_loaded"), sem("gb_loaded"), sem("gb2_loaded")
        rpb_loaded, rpb_stored, bias_loaded = sem("rpb_loaded"), sem("rpb_stored"), sem("bias_loaded")
        swapped = sem("swapped")
        pstep, vstep, astep = sem("pool_step"), sem("vector_step"), sem("scalar_step")
        consts_ready, bias_ready = sem("consts_ready"), sem("bias_ready")
        blk_zeroed, pad_zeroed = sem("blk_zeroed"), sem("pad_zeroed")
        angle_ready, trig_ready = sem("angle_ready"), sem("trig_ready")
        lam_dot, lam_exp = sem("lam_dot"), sem("lam_exp")
        squares, mean_sq, rstd_ready, xn_ready = sem("squares"), sem("mean_sq"), sem("rstd_ready"), sem("xn_ready")
        rot_ready, blk_ready, hidc_ready = sem("rot_ready"), sem("blk_ready"), sem("hidc_ready")
        max_ready, exp_ready, mixed_ready = sem("max_ready"), sem("exp_ready"), sem("mixed_ready")
        gate_ready, mg_ready, ya_ready, merged = sem("gate_ready"), sem("mg_ready"), sem("ya_ready"), sem("merged")
        sg_ready, hid_ready = sem("sg_ready"), sem("hid_ready")
        sig_ready, conv_ready, cent_ready, csq_ready = sem("sig_ready"), sem("conv_ready"), sem("cent_ready"), sem("csq_ready")
        std_ready, lnorm_ready, silu_ready, conv_mixed = sem("std_ready"), sem("lnorm_ready"), sem("silu_ready"), sem("conv_mixed")
        on_ready, x2_ready, yb_added = sem("on_ready"), sem("x2_ready"), sem("yb_added")
        ya_mean, ya_rstd = sem("ya_mean"), sem("ya_rstd")
        logit_max, logit_exp, aff_ready, top_ready, pick_ready = (sem("logit_max"), sem("logit_exp"), sem("aff_ready"),
                                                                 sem("top_ready"), sem("pick_ready"))
        gathered, xs_ready, glu_ready, h_ready = sem("gathered"), sem("xs_ready"), sem("glu_ready"), sem("h_ready")
        turned_x, hT_ready, eo0_ready, eo1_ready, spread_ready = (sem("turned_x"), sem("hT_ready"), sem("eo0_ready"),
                                                                  sem("eo1_ready"), sem("spread_ready"))
        y_done, y_read, out_ready, stored = sem("y_done"), sem("y_read"), sem("out_ready"), sem("stored")

        def pb(job):
            return bank[JOB[job] % BANKS]

        def is_full(eng, job):
            eng.wait_ge(full[JOB[job] % BANKS], JOB[job] // BANKS + 1)

        def is_read(eng, job):
            eng.wait_ge(free[JOB[job] % BANKS], JOB[job] // BANKS + 1)

        def bank_taken(eng, job):
            if JOB[job] >= BANKS:
                eng.wait_ge(free[JOB[job] % BANKS], JOB[job] // BANKS)

        def slot(ch):
            return ring[:, SLOT_OF[ch], :]

        def bcast(ap, dim, n):
            shape = list(ap.shape)
            shape.insert(dim, n)
            return ap.unsqueeze(dim).broadcast_to(shape)

        def gcol(name, k=0):
            return gain[:, GAIN_ROWS[name][0] + k:GAIN_ROWS[name][0] + k + 1]

        class Sent:

            def __init__(self, eng):
                self.eng, self.count, self.last = eng, {}, None

            def __call__(self, ins, sem_):
                key = id(sem_)
                self.count[key] = self.count.get(key, 0) + 1
                self.last = (sem_, self.count[key])
                ins.then_inc(sem_, 1)

            def bank(self, ins, job):
                b = JOB[job] % BANKS
                self.last = (free[b], JOB[job] // BANKS + 1)
                ins.then_inc(free[b], 1)

            def own(self):
                if self.last:
                    self.eng.wait_ge(*self.last)

        RPB = nc.dram_tensor("rpb_rows", (NH2 * 7, GRID, P), F32).ap()

        def kt(ap):
            return ap.rearrange("(k p) n -> p k n", p=P)

        def source(ch):
            kind, s = ch[0], slot(ch)
            if kind == "w_in":
                c0, n = W_IN_CUTS[ch[1]]
                return [(s[:, 0:KD * n].rearrange("p (k n) -> p k n", k=KD), kt(A["w_in"][0])[:, :, c0:c0 + n])]
            if kind == "cmp":
                w = A[("cmp_k_w1", "cmp_v_w1")[ch[1]]][0]
                return [(s.rearrange("p (k n) -> p k n", k=LP), kt(w))]
            if kind in ("bra", "brb"):
                w = A["w_branch_a" if kind == "bra" else "w_branch_b"][0]
                return [(s.rearrange("p (k n) -> p k n", k=4), kt(w))]
            if kind in ("wo", "wo2", "w_in2"):
                w = A[{"wo": "w_out", "wo2": "w_out_2", "w_in2": "w_in_2"}[kind]][0]
                return [(s.rearrange("p (k n) -> p k n", k=KD), kt(w)[:, :, ch[1] * NB:(ch[1] + 1) * NB])]
            if kind == "gu":
                d = s.rearrange("p (k v n) -> p k v n", k=KD, v=2)
                return [(d[:, :, v, :], kt(A[w][0])[:, :, ch[1] * GU:(ch[1] + 1) * GU])
                        for v, w in enumerate(("w_gate", "w_up"))]
            n = min(4, FK - 4 * ch[1])
            return [(s[:, 0:n * D].rearrange("p (k n) -> p k n", k=n),
                     kt(A["w_down"][0])[:, 4 * ch[1]:4 * ch[1] + n, :])]

        block = ctx.enter_context(nc.Block())

        LOADS = {}
        tot = [0] * SLOTS
        for ch in CHUNKS:
            tot[SLOT_OF[ch]] += 2 if ch[0] == "gu" else 1
            LOADS[ch] = tot[SLOT_OF[ch]]
        BASE = list(tot)

        def has_weights(eng, ch):
            eng.wait_ge(loaded[SLOT_OF[ch]], 16 * LOADS[ch])

        @block.sync
        def _(sp):
            sp.dma_start(X[:, :, :], A["x"][0].rearrange("(t p) d -> p t d", p=P)).then_inc(x_loaded, 16)
            owner = {}
            for ch in CHUNKS:
                s = SLOT_OF[ch]
                if s in owner:
                    prev = owner[s]
                    if prev[0] == "down" and prev[1] < 5:
                        sp.wait_ge(down_used, prev[1] + 1)
                    else:
                        is_full(sp, LAST_USE[prev])
                elif s >= 5:
                    is_read(sp, ("wo", 1, 1, 0))
                owner[s] = ch
                for dst, src in source(ch):
                    sp.dma_start(dst, src).then_inc(loaded[s], 16)
                if ch == ("gu", 4):
                    is_read(sp, ("wo", 1, 1, 0))
                    sp.wait_ge(rpb_stored, 16)
                    for q in range(2):
                        for h in range(NH2):
                            src = bass.AP(tensor=RPB.tensor, offset=(h * 7 + 1 - q) * GRID * P + GRID - 1,
                                          ap=[[P - 1, GRID], [GRID * P, 6], [1, GRID]])
                            sp.dma_start(bias[GRID * q:GRID * (q + 1), h, :, :], src).then_inc(bias_loaded, 16)

            wg = A["w_gate_2"][0].rearrange("e (k p) f -> e p k f", p=P)
            wu = A["w_up_2"][0].rearrange("e (k p) f -> e p k f", p=P)
            wd = A["w_down_2"][0].rearrange("e (j c p) f -> e p c j f", j=FJ, p=P)

            def load_expert(e, q, s):
                if q < 8:
                    w = wg if q < 4 else wu
                    src = w[e, :, 2 * (q % 4):2 * (q % 4) + 2, :].rearrange("o p k f -> (o p) k f")
                    dst = ring[:, s, :].rearrange("p (k f) -> p k f", k=2)
                else:
                    src = wd[e, :, q - 8, :, :].rearrange("o p k f -> (o p) k f")
                    dst = ring[:, s, :].rearrange("p (k f) -> p k f", k=4)
                sp.dma_start(dst, src).then_inc(loaded[s], 16)

            for n in range(2 * XCH):
                s, o = n % SLOTS, n // SLOTS
                if o:
                    sp.wait_ge(used[s], o)
                elif s == SLOTS - 1:
                    sp.wait_ge(conv_mixed, CT)
                else:
                    is_full(sp, LAST_USE[owner[s]])
                load_expert(slice(n // XCH, n // XCH + 1), n % XCH, s)
            with sp.Fori(1, E // 2) as it:
                for n in range(2 * XCH):
                    s, o = n % SLOTS, n // SLOTS
                    sp.wait_ge(used[s], it * 3 + o)
                    if n < XCH:
                        load_expert(bass.ds(it * 2, 1), n % XCH, s)
                    else:
                        load_expert(bass.ds(it * 2 + 1, 1), n % XCH, s)
            for t in range(T):
                sp.wait_ge(out_ready, t + 1)
                sp.dma_start(out[0].rearrange("(t p) d -> p t d", p=P)[:, t, :], UTf[:, t, :]).then_inc(stored, 16)
            sp.wait_ge(stored, 16 * T)


        @block.gpsimd
        def _(pool):
            g = nc.gpsimd
            sent = Sent(pool)

            def link(ins):
                sent(ins, pstep)
                sent.own()

            for i in range(HALF):
                g.memset(inv_freq[:, i:i + 1], float(np.float32(1.0) / np.float32(THETA ** (2 * i / DH))))
            g.memset(ones[:, :], 1.0)
            g.memset(mhalf[:, :], -0.5)
            g.memset(eps_col[:, :], EPS)
            g.memset(ident[:, :], 0.0)
            g.memset(causal[:, :], 0.0)
            g.memset(cmp_add[:, :, :], 0.0)
            g.memset(cmp_keep[:, :, :], 1.0)
            g.memset(delta[:, :, :], 1.0)
            g.memset(rpbp[:, :], 0.0)
            g.iota(tok_int[:, :], [[1, S]], base=0, channel_multiplier=0)
            link(g.iota(part_int[:, :], [[P, T]], base=0, channel_multiplier=1))
            g.affine_select(out=ident[:, :], in_=ident[:, :], compare_op=ALU.not_equal, fill=1.0, base=0,
                            pattern=[[-1, P]], channel_multiplier=1)
            g.affine_select(out=causal[:, P:S], in_=causal[:, P:S], compare_op=ALU.is_ge, fill=NEG, base=0,
                            pattern=[[-1, P]], channel_multiplier=1)
            for m, fill in ((cmp_add, NEG), (cmp_keep, 0.0)):
                g.affine_select(out=m[:, :, :], in_=m[:, :, :], compare_op=ALU.is_ge, fill=fill, base=1 - CMP_LEN,
                                pattern=[[P, T], [-CMP_STRIDE, 16]], channel_multiplier=1)
            sent(g.affine_select(out=delta[:, :, :], in_=delta[:, :, :], compare_op=ALU.is_equal, fill=0.0, base=0,
                            pattern=[[1, E], [0, CAP]], channel_multiplier=-1), consts_ready)
            sent(g.memset(blk[:, :, :, :, :], 0.0), blk_zeroed)

            def power(k, out_, in_, ready, done, count, w):
                sent.own()
                pool.wait_ge(ready, count)
                sent(g.tensor_tensor(out_, in_, mhalf[:, 0:w], ALU.pow), done)

            def rstd(i):
                power(i, stat[:, 8 * i + 4:8 * i + 4 + T], stat[:, 8 * i + 2:8 * i + 2 + T], mean_sq, rstd_ready, i + 1, T)

            pool.wait_ge(consts_ready, 1)
            rstd(0)
            power(0, ystat[:, 8:16], ystat[:, 0:8], ya_mean, ya_rstd, 1, 8)
            rstd(1)
            is_read(pool, ("wo", 1, 1, 0))
            g.memset(upad[:, :, 0:PAD], 0.0)
            sent(g.memset(upad[:, :, PAD + S:], 0.0), pad_zeroed)
            pool.wait_ge(bias_loaded, 16 * 2 * NH2)
            for q in range(2):
                b = bias[GRID * q:GRID * (q + 1), :, :, :].rearrange("p h d c -> p (h d) c")
                sent.own()
                hi = b[:, :, 0:GRID - WIN_C]
                lo = b[:, :, WIN_C:GRID]
                link(g.affine_select(out=hi, in_=hi, compare_op=ALU.is_ge, fill=NEG, base=WIN_C // 2,
                                     pattern=[[0, 6 * NH2], [1, GRID - WIN_C]], channel_multiplier=-1))
                last = g.affine_select(out=lo, in_=lo, compare_op=ALU.is_ge, fill=NEG, base=WIN_C // 2 - 1 - WIN_C,
                                       pattern=[[0, 6 * NH2], [-1, GRID - WIN_C]], channel_multiplier=1)
                sent(last, bias_ready)
            for i in range(2, 7):
                rstd(i)

        @block.scalar
        def _(act):
            a = nc.scalar
            sent = Sent(act)

            r0 = 0
            for name in ("attn_norm_g", "ffn_norm_g", "norm1_g_2", "norm2_g_2", "attn_out_g_2", "conv_out_g_2",
                         "conv_b_2", "conv_ln_g_2", "conv_ln_b_2", "diff_subln_g"):
                w = A[name][0].rearrange("(r c) -> r c", c=P)
                act.dma_start(SC[r0:r0 + w.shape[0], 0, 0:P], w).then_inc(rows_loaded, 16)
                r0 += w.shape[0]
            for name in ("cmp_pe_k", "cmp_pe_v"):
                act.dma_start(SC[r0:r0 + LP, 0, 0:P], A[name][0].rearrange("(r l) d -> r (l d)", l=2)).then_inc(rows_loaded, 16)
                r0 += LP
            act.dma_start(SC[0:TAPS * CT, 0, P:2 * P], A["conv_w_2"][0].rearrange("k (c n) -> (k c) n", n=P)).then_inc(conv_loaded, 16)
            act.dma_start(pos_int[:, :], A["positions"].rearrange("a (t p) -> p (a t)", p=P),
                          allow_slow_non_contiguous=True).then_inc(small_loaded, 16)
            act.dma_start(dl[:, :, :], A["diff_lambda"][0].rearrange("(o r) d -> o r d", o=1).broadcast_to([P, 4, DH])).then_inc(small_loaded, 16)
            act.dma_start(w_r[:, :, :], kt(A["w_router_2"][0])).then_inc(small_loaded, 16)
            for v, name in enumerate(("cmp_k_w2", "cmp_v_w2")):
                act.dma_start(w2[:, v, :, :], kt(A[name][0])).then_inc(small_loaded, 16)
            act.dma_start(GB[:, :], A["final_norm_g"].rearrange("(o d) -> o d", o=1).broadcast_to([P, D])).then_inc(gb_loaded, 16)
            act.wait_ge(consts_ready, 1)
            for h in range(NH2):
                act.dma_start(rpbp[7 * h:7 * h + 7, GRID - WIN_C:GRID - WIN_C + RPB_C],
                              A["rpb_2"][0][h, RPB_R // 2 - 3:RPB_R // 2 + 4, :]).then_inc(rpb_loaded, 16)

            def squares_of(i, src, junk):
                for t in range(T):
                    if i == 0 and t == 0:
                        act.wait_ge(x_loaded, 16)
                    if i == 1:
                        is_read(act, ("wo", 1, 1, 0))
                    if i == 2:
                        is_read(act, ("down", 2 * t + 1))
                    if i == 3:
                        act.wait_ge(x2_ready, t + 1)
                    if i == 4 and t == 0:
                        is_read(act, ("PV", NU1 + 2, 0))
                    if i == 4 and t == 1:
                        is_read(act, ("PV", NU1 + 3, 0))
                    if i == 5:
                        is_read(act, ("wo2", 1, 1, 0))
                    if i == 6:
                        act.wait_ge(y_read, 4)
                    sent(a.activation(junk[:, t, :], src[:, t, :], ACT.Square,
                                 accum_out=stat[:, 8 * i + t:8 * i + t + 1]), squares)

            def read(job, out_, in_, f=ACT.Copy, **kw):
                is_full(act, job)
                sent.bank(a.activation(out_, in_, f, **kw), job)

            def features(job, k0, name):
                is_full(act, job)
                for kk in range(2):
                    ins = a.activation(UT[:, k0 + kk, :], pb(job)[:, kk * S:(kk + 1) * S], ACT.Copy,
                                       scale=gcol(name, k0 + kk) if name else 1.0)
                sent.bank(ins, job)

            for st in STEPS:
                kind = st[0]
                sent.own()
                job = st + (0,)
                if kind == "norm":
                    i = {0: 0, 1: 1, 2: 2, 3: 5}[st[1]]
                    squares_of(i, X, UTf)
                    if i == 0:
                        act.wait_ge(rpb_loaded, 16 * NH2)
                        act.dma_start(RPB, bcast(rpbp[0:7 * NH2, :], 1, GRID)).then_inc(rpb_stored, 16)
                        act.wait_ge(angle_ready, 1)
                        sent(a.activation(trig[:, 0:2, :, :], trig[:, 0:2, :, :], ACT.Sin), trig_ready)
                        act.wait_ge(lam_dot, 1)
                        sent(a.activation(lamv[:, 2:4], lamv[:, 0:2], ACT.Exp), lam_exp)
                        is_read(act, ("gains", 0))
                    if i == 2:
                        squares_of(3, X, UTf)
                    name = ("attn", "ffn", "norm1", "norm2")[st[1]]
                    for q in (0, 2):
                        features(st + (q,), 2 * q, name)
                elif kind == "proj":
                    _, c, t = st
                    if c == DV:
                        read(job, vdiff[:, t, :], pb(job)[:, :])
                    elif c >= MG0:
                        read(job, mg[:, t, (c - MG0) * NB:(c - MG0 + 1) * NB], pb(job)[:, :])
                elif kind == "rot":
                    _, c, t = st
                    b0, nb = {DQ: (0, 4), DK: (4, 4), NQ: (8, 4), KV4: (12, 3), KV2: (15, 1)}[c]
                    read(job, qkT[:, b0:b0 + nb, t * P:(t + 1) * P],
                         pb(job)[:, 0:nb * P].rearrange("p (b s) -> p b s", b=nb))
                elif kind == "blocks":
                    for t in range(T):
                        is_read(act, ("rot", KV4, t, 0))
                    for g_ in range(2):
                        act.dma_start(kswap[DH * (1 - g_):DH * (2 - g_), :, :],
                                      qkT[DH * g_:DH * (g_ + 1), 12:14, :]).then_inc(swapped, 16)
                    for t in range(T):
                        is_read(act, ("proj", KV2, t, 0))
                    sent(a.activation(ngate[:, :, :, :], ngate[:, :, :, :], ACT.Sigmoid), gate_ready)
                elif kind == "cmph":
                    read(job, hidc[0:64, :], pb(job)[0:64, 0:CH], ACT.Silu)
                elif kind == "cmpt":
                    read(job, hidcT[:, :, 0:64], pb(job)[:, 0:2 * 64].rearrange("p (k c) -> p k c", k=2))
                elif kind == "S":
                    u = st[1]
                    k, _, t = UNITS[u]
                    sbuf = (probs1 if u < NU1 else probs2)[:, u % 2]
                    act.wait_ge(max_ready, u + 1)
                    if k == "cmp":
                        v = sbuf.rearrange("p m k -> p (m k)")[:, 0:8 * 16].rearrange("p (n i) -> p n i", n=8)
                        sent(a.activation(v[:, :, 0:NCB], v[:, :, 0:NCB], ACT.Exp), exp_ready)
                    else:
                        w = key_tiles(u) * P
                        for m in range(4):
                            ins = a.activation(sbuf[:, m, 0:w], sbuf[:, m, 0:w], ACT.Exp, bias=nmax[:, u, m:m + 1],
                                               accum_out=rsum[:, u, m:m + 1])
                        sent(ins, exp_ready)
                elif kind == "PT":
                    u = st[1]
                    k, _, t = UNITS[u]
                    tb = (turned1 if u < NU1 else turned2)[:, u % 2]
                    if u >= 2:
                        is_full(act, ("PV", u - 2, 0))
                    rows = NCB if k == "cmp" else P
                    cols = (2 if k == "diff" else 4) * key_tiles(u) * P // turns(u) if k != "cmp" else NB
                    for j in range(turns(u)):
                        read(st + (j,), tb[0:rows, j * NB:j * NB + cols], pb(st + (j,))[0:rows, 0:cols])
                elif kind == "mgs":
                    is_read(act, ("proj", 9, 1, 0))
                    is_read(act, ("proj", 9, 0, 0))
                    sent(a.activation(mg[:, :, :], mg[:, :, :], ACT.Sigmoid), mg_ready)
                elif kind in ("yaT", "ybT"):
                    dst = yaT if kind == "yaT" else ybT
                    for t in range(T):
                        j = st + (t,)
                        read(j, dst[:, :, t * P:(t + 1) * P], pb(j)[:, :].rearrange("p (b s) -> p b s", b=4),
                             scale=subln[:, 0:1] if kind == "yaT" else 1.0)
                elif kind == "mT":
                    for q in (0, 2):
                        features(st + (q,), 2 * q, None)
                elif kind == "gu":
                    n = 2 * st[1] + st[2]
                    is_full(act, job)
                    if n >= 2:
                        is_read(act, ("gu", (n - 2) // 2, n % 2, 0))
                    sent(a.activation(sgate[:, n % 2], pb(job)[:, 0:GU], ACT.Silu), sg_ready)
                elif kind == "hT":
                    c = st[1]
                    read(job, hidT[:, 2 * c:2 * c + 2, :].rearrange("p k s -> p (k s)"), pb(job)[:, :])
                elif kind == "qk":
                    _, c, h = st
                    read(job, qkT2[:, 4 * c + 2 * h:4 * c + 2 * h + 2, :].rearrange("p k s -> p (k s)"), pb(job)[:, :])
                elif kind == "v":
                    read(job, v2[:, st[1], :], pb(job)[:, :])
                elif kind == "ag":
                    _, c, h = st
                    src = pb(job)[:, :].rearrange("p (k s) -> p k s", k=2)
                    if c == 0:
                        read(job, upad[:, 2 * h:2 * h + 2, PAD:PAD + S], src)
                    else:
                        read(job, dw[:, 2 * h:2 * h + 2, :], src, ACT.Sigmoid)
                elif kind == "on":
                    squares_of(4, o2, cz_.rearrange("p (t c) -> p t c", t=T))
                elif kind == "oT":
                    for t in range(T):
                        j = st + (t,)
                        is_full(act, j)
                        for k in range(4):
                            ins = a.activation(UT[:, k, t * P:(t + 1) * P], pb(j)[:, k * P:(k + 1) * P], ACT.Copy,
                                               scale=gcol("attn_out", k))
                        sent.bank(ins, j)
                    act.dma_start(GB[:, :], A["final_g_2"].rearrange("(o d) -> o d", o=1).broadcast_to([P, D])).then_inc(gb2_loaded, 16)
                elif kind == "cvar":
                    is_read(act, ("cmean", 0))
                    sent(a.activation(cz[:, :, :], dw[:, :, :], ACT.Square), csq_ready)
                    read(job, crs, pb(job)[:, 0:S], ACT.Sqrt, bias=eps_col[:, 0:1], scale=1.0 / CW)
                    act.wait_ge(lnorm_ready, 1)
                    for c in range(CT):
                        sent(a.activation(cz[:, c, :], dw[:, c, :], ACT.Silu, bias=gcol("ln_b", c),
                                     scale=gcol("ln_g", c)), silu_ready)
                elif kind == "crms":
                    act.wait_ge(silu_ready, CT)
                    sent(a.activation(dw[:, :, :], cz[:, :, :], ACT.Square), csq_ready)
                    read(job, crs, pb(job)[:, 0:S], ACT.Sqrt, bias=eps_col[:, 0:1], scale=1.0 / CW)
                elif kind == "logit":
                    is_read(act, job)
                    sent(a.activation(affs_[:, 0:T * E], affs_[:, 0:T * E], ACT.Exp), logit_exp)

            with act.Fori(0, E // 2) as it:
                for x in range(2):
                    n = it * 2 + (x + 1)
                    q = x * XCH + 3
                    act.wait_ge(used[q % SLOTS], it * 3 + q // SLOTS + 1)
                    a.activation(sgx, bank[4][:, :], ACT.Silu).then_inc(glu_ready, 1)
                    act.wait_ge(turned_x, n)
                    a.activation(hidxT_, bank[4][:, :], ACT.Copy).then_inc(hT_ready, 1)
                    q = x * XCH + XCH - 1
                    act.wait_ge(used[q % SLOTS], it * 3 + q // SLOTS + 1)
                    a.activation(eo[:, 0, :], bank[6][:, :], ACT.Copy).then_inc(eo0_ready, 1)
            squares_of(6, SC, UTf)

        @block.vector
        def _(dve):
            v = nc.vector
            sent = Sent(dve)
            freed = sent.bank

            def link(ins):
                sent(ins, vstep)
                sent.own()

            def read(job, out_, in_):
                is_full(dve, job)
                freed(v.tensor_copy(out_, in_), job)

            def features(job, k0, name):
                is_full(dve, job)
                for kk in range(2):
                    src = pb(job)[:, kk * S:(kk + 1) * S]
                    if name:
                        ins = v.tensor_scalar(UT[:, k0 + kk, :], src, gcol(name, k0 + kk), None, ALU.mult)
                    else:
                        ins = v.tensor_copy(UT[:, k0 + kk, :], src)
                freed(ins, job)

            def mean_of(i, width):
                dve.wait_ge(squares, T * (i + 1))
                sent(v.tensor_scalar(stat[:, 8 * i + 2:8 * i + 2 + T], stat[:, 8 * i:8 * i + T], 1.0 / width, EPS,
                                ALU.mult, ALU.add), mean_sq)
                dve.wait_ge(rstd_ready, i + 1)

            def rcol(i, t):
                return stat[:, 8 * i + 4 + t:8 * i + 5 + t]

            def angles():
                dve.wait_ge(small_loaded, 16 * 5)
                dve.wait_ge(consts_ready, 1)
                v.tensor_copy(tok_free[:, :], tok_int[:, :])
                v.tensor_copy(tok_part[:, :], part_int[:, :])
                link(v.tensor_copy(pos[:, :], pos_int[:, :]))
                for t in range(T):
                    ins = v.tensor_scalar(ang[:, t * HALF:(t + 1) * HALF], inv_freq[:, :], pos[:, t:t + 1], None, ALU.mult)
                link(ins)
                big = 1.5 * 2.0 ** 23
                two_pi = [6.28125, float(np.float32(0.00193500518798828125)), 0.0]
                two_pi[2] = 2 * math.pi - two_pi[0] - two_pi[1]
                link(v.tensor_scalar(angk[:, :], ang[:, :], 1 / (2 * math.pi), big, ALU.mult, ALU.add))
                link(v.tensor_scalar(angk[:, :], angk[:, :], big, None, ALU.subtract))
                for c in two_pi:
                    link(v.scalar_tensor_tensor(ang[:, :], angk[:, :], -c, ang[:, :], ALU.mult, ALU.add))
                lim = 3.1415925
                s_ = trig[:, 0, :, :].rearrange("p t i -> p (t i)")
                c_ = trig[:, 1, :, :].rearrange("p t i -> p (t i)")
                link(v.tensor_scalar(ang[:, :], ang[:, :], 0.0, None, ALU.add))
                v.tensor_scalar(s_, ang[:, :], lim, -lim, ALU.min, ALU.max)
                link(v.tensor_scalar(angk[:, :], ang[:, :], math.pi / 2, -2 * math.pi, ALU.is_gt, ALU.mult))
                link(v.scalar_tensor_tensor(ang[:, :], ang[:, :], math.pi / 2, angk[:, :], ALU.add, ALU.add))
                sent(v.tensor_scalar(c_, ang[:, :], lim, -lim, ALU.min, ALU.max), angle_ready)

            def lam():
                d2 = dl[:, :, :].rearrange("p (a b) d -> p a b d", b=2)
                link(v.tensor_tensor(dlp[:, :, :], d2[:, :, 0, :], d2[:, :, 1, :], ALU.mult))
                sent(v.tensor_reduce(lamv[:, 0:2], dlp[:, :, :], AX_X, ALU.add), lam_dot)

            def neg_lam():
                dve.wait_ge(lam_exp, 1)
                link(v.tensor_tensor(lamv[:, 4:5], lamv[:, 3:4], lamv[:, 2:3], ALU.subtract))
                link(v.tensor_scalar(lamv[:, 5:6], lamv[:, 4:5], -LAM_INIT, None, ALU.add))
                dve.wait_ge(trig_ready, 1)
                link(v.tensor_scalar(trig[:, 2, :, :], trig[:, 0, :, :], -1.0, None, ALU.mult))

            def rope(src, dst, t, heads, off):
                a3 = rope_a[:, off:off + heads * DH].rearrange("p (n r) -> p n r", r=HALF)
                x3 = src.rearrange("p (n r) -> p n r", r=HALF)
                v.tensor_tensor(a3, x3, bcast(trig[:, 1, t, :], 1, 2 * heads), ALU.mult)
                b4 = rope_b[:, off:off + heads * DH].rearrange("p (n h r) -> p n h r", h=2, r=HALF)
                x4 = src.rearrange("p (n h r) -> p n h r", h=2, r=HALF)
                v.tensor_tensor(b4[:, :, 0, :], x4[:, :, 1, :], bcast(trig[:, 2, t, :], 1, heads), ALU.mult)
                return v.tensor_tensor(b4[:, :, 1, :], x4[:, :, 0, :], bcast(trig[:, 0, t, :], 1, heads), ALU.mult)

            ROTS = [st[1:] for st in STEPS if st[0] == "rot"]

            def softmax_scale(u, k):
                link(v.reciprocal(rinv[:, u, 0:k], rsum[:, u, 0:k]))

            def scores(u):
                kind, p, t = UNITS[u]
                sbuf = (probs1 if u < NU1 else probs2)[:, u % 2]
                if u >= 2:
                    is_full(dve, ("PT", u - 2, turns(u - 2) - 1))
                if kind == "cmp":
                    sv = sbuf.rearrange("p m k -> p (m k)")[:, 0:8 * 16].rearrange("p (n i) -> p n i", n=8)
                    for s in range(2):
                        job = ("S", u, s)
                        is_full(dve, job)
                        freed(v.scalar_tensor_tensor(
                            sv[:, 4 * s:4 * s + 4, 0:NCB], pb(job)[:, 0:64].rearrange("p (n i) -> p n i", n=4)[:, :, 0:NCB],
                            SCALE, bcast(cmp_add[:, t, 0:NCB], 1, 4), ALU.mult, ALU.add), job)
                    is_read(dve, ("S", u, 0))
                    is_read(dve, ("S", u, 1))
                    link(v.tensor_reduce(nmax[:, u, 0:8], sv[:, :, 0:NCB], AX_X, ALU.max, negate=True))
                    sent(v.tensor_tensor(sv[:, :, 0:NCB], sv[:, :, 0:NCB], bcast(nmax[:, u, 0:8], 2, NCB),
                                    ALU.add), max_ready)
                    return
                w = key_tiles(u) * P
                if kind == "grid":
                    dve.wait_ge(bias_ready, 2)
                for s in range(2):
                    job = ("S", u, s)
                    if kind == "grid":
                        m = bias.rearrange("p h d c -> p h (d c)")[:, 4 * p + s:4 * p + s + 3:2, (2 - 2 * t) * GRID:(6 - 2 * t) * GRID]
                    else:
                        m = bcast(causal[:, S - w:S], 1, 2)
                    is_full(dve, job)
                    freed(v.scalar_tensor_tensor(
                        sbuf[:, 2 * s:2 * s + 2, 0:w], pb(job)[:, :].rearrange("p (m k) -> p m k", m=2)[:, :, 0:w],
                        SCALE, m, ALU.mult, ALU.add), job)
                is_read(dve, ("S", u, 0))
                is_read(dve, ("S", u, 1))
                sent(v.tensor_reduce(nmax[:, u, 0:4], sbuf[:, :, 0:w], AX_X, ALU.max, negate=True), max_ready)

            def after_exp(u):
                kind, p, t = UNITS[u]
                sbuf = probs1[:, u % 2]
                if kind == "diff":
                    dve.wait_ge(exp_ready, u + 1)
                    w = key_tiles(u) * P
                    softmax_scale(u, 4)
                    link(v.tensor_scalar(rinv[:, u, 2:4], rinv[:, u, 2:4], lamv[:, 5:6], None, ALU.mult))
                    for i in range(2):
                        ins = v.tensor_scalar(sbuf[:, 2 + i, 0:w], sbuf[:, 2 + i, 0:w], rinv[:, u, 2 + i:3 + i], None, ALU.mult)
                    link(ins)
                    for i in range(2):
                        ins = v.scalar_tensor_tensor(sbuf[:, i, 0:w], sbuf[:, i, 0:w], rinv[:, u, i:i + 1],
                                                     sbuf[:, 2 + i, 0:w], ALU.mult, ALU.add)
                    sent(ins, mixed_ready)
                elif kind == "cmp":
                    dve.wait_ge(exp_ready, u + 1)
                    sv = sbuf.rearrange("p m k -> p (m k)")[:, 0:8 * 16].rearrange("p (n i) -> p n i", n=8)
                    v.tensor_reduce(rsum[:, u, 0:8], sv[:, :, 0:NCB], AX_X, ALU.add)
                    sent(v.tensor_tensor(sv[:, :, 0:NCB], sv[:, :, 0:NCB], bcast(cmp_keep[:, t, 0:NCB], 1, 8),
                                    ALU.mult), mixed_ready)
                    dve.wait_ge(mixed_ready, u + 1)

            added = [0]

            def outputs(u):
                kind, p, t = UNITS[u]
                job = ("PV", u, 0)
                if kind == "diff":
                    read(job, ya[:, t, 2 * P * p:2 * P * (p + 1)], pb(job)[:, 0:2 * P])
                    return
                dve.wait_ge(exp_ready, u + 1)
                if kind == "cmp":
                    dve.wait_ge(gate_ready, 1)
                    softmax_scale(u, 8)
                    link(v.tensor_tensor(rinv[:, u, :], rinv[:, u, :], ngate[:, t, 0, :], ALU.mult))
                    is_full(dve, job)
                    freed(v.tensor_tensor(yb[:, t, :].rearrange("p (n r) -> p n r", n=8),
                                          pb(job)[:, :].rearrange("p (n r) -> p n r", n=8),
                                          bcast(rinv[:, u, :], 2, DH), ALU.mult), job)
                    is_read(dve, job)
                    return
                softmax_scale(u, 4)
                o3 = pb(job)[:, 0:4 * DH].rearrange("p (m r) -> p m r", m=4)
                if kind == "grid":
                    is_full(dve, job)
                    dst = o2[:, t, :].rearrange("p (b s r) -> p s b r", s=2, r=DH)[:, :, 2 * p:2 * p + 2, :]
                    freed(v.tensor_tensor(dst, o3.rearrange("p (s i) r -> p s i r", s=2),
                                          bcast(rinv[:, u, 0:4], 2, DH).rearrange("p (s i) r -> p s i r", s=2), ALU.mult), job)
                    return
                br = 1 if kind == "sel" else 2
                gt = ngate[:, t, br, :].rearrange("p (g b) -> p g b", g=2)[:, :, 2 * p:2 * p + 2]
                r2 = rinv[:, u, 0:4].rearrange("p (g b) -> p g b", g=2)
                link(v.tensor_tensor(r2, r2, gt, ALU.mult))
                tmp = scf[:, 0:4 * DH].rearrange("p (m r) -> p m r", m=4)
                is_full(dve, job)
                freed(v.tensor_tensor(tmp, o3, bcast(rinv[:, u, 0:4], 2, DH), ALU.mult), job)
                is_read(dve, job)
                dst = yb[:, t, :].rearrange("p (g b r) -> p g b r", g=2, r=DH)[:, :, 2 * p:2 * p + 2, :]
                sent(v.tensor_tensor(dst, dst, tmp.rearrange("p (g b) r -> p g b r", g=2), ALU.add), yb_added)
                added[0] += 1
                dve.wait_ge(yb_added, added[0])

            for st in STEPS:
                kind = st[0]
                sent.own()
                job = st + (0,)
                if kind == "gains":
                    read(("gains", 0), gain[:, 0:GAINS], pb(("gains", 0))[:, 0:GAINS])
                    read(("gains", 1), convw[:, :, :].rearrange("p k c -> p (k c)"), pb(("gains", 1))[:, 0:TAPS * CT])
                    is_read(dve, ("gains", 0))
                    is_read(dve, ("gains", 1))
                elif kind == "norm":
                    k = st[1]
                    i = {0: 0, 1: 1, 2: 2, 3: 5}[k]
                    mean_of(i, D)
                    if k == 2:
                        dve.wait_ge(gb_loaded, 16)
                        for t in range(T):
                            sent(v.scalar_tensor_tensor(X[:, t, :], X[:, t, :], rcol(2, t), GB[:, :], ALU.mult,
                                                   ALU.mult), x2_ready)
                        dve.wait_ge(x2_ready, T)
                        i = 3
                        mean_of(i, D)
                    for t in range(T):
                        sent(v.tensor_scalar(SC[:, t, :], X[:, t, :], rcol(i, t), None, ALU.mult), xn_ready)
                    if k == 0:
                        angles()
                        lam()
                        neg_lam()
                        v.tensor_scalar(subln[:, :], gcol("subln"), 1.0 - LAM_INIT, None, ALU.mult)
                    for q in (1, 3):
                        features(st + (q,), 2 * q, ("attn", "ffn", "norm1", "norm2")[k])
                elif kind == "proj" and st[1] in (DQ, DK, NQ, KV4, KV2):
                    _, c, t = st
                    r = ROTS.index((c, t))
                    buf = rot[:, r % 2]
                    is_full(dve, job)
                    if r < 2:
                        is_full(dve, ("norm", 0, 3))
                    else:
                        is_full(dve, ("rot",) + ROTS[r - 2] + (0,))
                    if c in (DQ, DK, NQ):
                        link(rope(pb(job)[:, :], buf, t, 8, 0))
                        if c == NQ:
                            o = buf.rearrange("p (b g r) -> p g b r", g=2, r=DH)
                            x1, x2 = (z.rearrange("p (g b r) -> p g b r", g=2, r=DH) for z in (rope_a, rope_b))
                            sent(v.tensor_tensor(o, x1, x2, ALU.add), rot_ready)
                        else:
                            sent(v.tensor_tensor(buf, rope_a, rope_b, ALU.add), rot_ready)
                        freed(v.tensor_copy(lamv[:, 6:7], pb(job)[:, 0:1]), job)
                    elif c == KV4:
                        rope(pb(job)[:, 0:P], buf, t, 2, 0)
                        rope(pb(job)[:, 2 * P:3 * P], buf, t, 2, 2 * P)
                        v.tensor_copy(buf[:, P:2 * P], pb(job)[:, P:2 * P])
                        freed(v.tensor_copy(vsel[:, t, :], pb(job)[:, 3 * P:4 * P]), job)
                        is_read(dve, job)
                        o, x1, x2 = (z.rearrange("p (a b) -> p a b", b=2 * P)[:, :, 0:P] for z in (buf, rope_a, rope_b))
                        sent(v.tensor_tensor(o, x1, x2, ALU.add), rot_ready)
                    else:
                        rope(pb(job)[:, 0:P], buf, t, 2, 0)
                        v.tensor_copy(vwin[:, t, :], pb(job)[:, P:2 * P])
                        freed(v.tensor_copy(ngate[:, t, :, :].rearrange("p b h -> p (b h)"), pb(job)[:, 2 * P:2 * P + 24]), job)
                        is_read(dve, job)
                        sent(v.tensor_tensor(buf[:, 0:P], rope_a[:, 0:P], rope_b[:, 0:P], ALU.add), rot_ready)
                elif kind == "blocks":
                    dve.wait_ge(swapped, 32)
                    dve.wait_ge(blk_zeroed, 1)
                    for t in range(T):
                        is_read(dve, ("rot", KV4, t, 0))
                    for kv in range(2):
                        pe0 = GAIN_ROWS[("pe_k", "pe_v")[kv]][0]
                        for hf in range(2):
                            for g in range(2):
                                src = (qkT[:, 12 + kv, :] if g == hf else kswap[:, kv, :])[DH * hf:DH * hf + DH, :]
                                win = bass.AP(tensor=src.tensor, offset=src.offset + hf,
                                              ap=[list(src.ap[0]), [2, LP], [CMP_STRIDE, NCB]])
                                pe_ = bcast(gain[DH * hf:DH * hf + DH, pe0:pe0 + LP], 2, NCB)
                                ins = v.tensor_tensor(blk[DH * hf:DH * hf + DH, kv, :, g, 0:NCB], win, pe_, ALU.add)
                    sent(ins, blk_ready)
                elif kind == "cmpw":
                    is_full(dve, job)
                    v.tensor_copy(kcT[:, :], pb(job)[:, 0:16])
                    freed(v.tensor_copy(vcs[0:16, :], pb(job)[0:16, 64:64 + 2 * DH]), job)
                elif kind == "S":
                    scores(st[1])
                elif kind == "PT":
                    if st[1] < NU1:
                        after_exp(st[1])
                elif kind == "PV":
                    outputs(st[1])
                elif kind == "yan":
                    for u in range(4):
                        is_read(dve, ("PV", u, 0))
                    sq = scf[:, 0:D]
                    link(v.tensor_tensor(sq, ya_, ya_, ALU.mult))
                    link(v.tensor_reduce(ystat[:, 0:8], sq.rearrange("p (n r) -> p n r", n=8), AX_X, ALU.add))
                    sent(v.tensor_scalar(ystat[:, 0:8], ystat[:, 0:8], 1.0 / P, EPS, ALU.mult, ALU.add), ya_mean)
                elif kind == "yas":
                    dve.wait_ge(ya_rstd, 1)
                    y3 = ya_.rearrange("p (n r) -> p n r", n=8)
                    sent(v.tensor_tensor(y3, y3, bcast(ystat[:, 8:16], 2, P), ALU.mult), ya_ready)
                elif kind == "bra":
                    _, t, h = st
                    m = mg[:, t, h * NB:(h + 1) * NB]
                    dve.wait_ge(mg_ready, 1)
                    is_full(dve, job)
                    freed(v.tensor_tensor(m, pb(job)[:, :], m, ALU.mult), job)
                elif kind == "brb":
                    _, t, h = st
                    o = SC[:, t, h * NB:(h + 1) * NB]
                    is_full(dve, job)
                    freed(v.tensor_tensor(o, pb(job)[:, :], mg[:, t, D + h * NB:D + (h + 1) * NB], ALU.mult), job)
                    is_read(dve, job)
                    is_read(dve, ("bra", t, h, 0))
                    sent(v.tensor_tensor(o, o, mg[:, t, h * NB:(h + 1) * NB], ALU.add), merged)
                elif kind == "mT":
                    for q in (1, 3):
                        features(st + (q,), 2 * q, None)
                elif kind in ("wo", "wo2"):
                    _, t, h = st
                    o = X[:, t, h * NB:(h + 1) * NB]
                    is_full(dve, job)
                    freed(v.tensor_tensor(o, pb(job)[:, :], o, ALU.add), job)
                elif kind == "gu":
                    _, c, t = st
                    k = 2 * c + t
                    dve.wait_ge(sg_ready, k + 1)
                    if c >= 2:
                        is_full(dve, ("hT", c - 2, 0))
                    freed(v.tensor_tensor(hid[:, k % 4], pb(job)[:, GU:2 * GU], sgate[:, k % 2], ALU.mult), job)
                elif kind == "down":
                    for q in range(4):
                        t, h = q // 2, q % 2
                        j = st + (q,)
                        o = X[:, t, h * NB:(h + 1) * NB]
                        is_full(dve, j)
                        freed(v.tensor_tensor(o, pb(j)[:, :], o, ALU.add), j)
                    for q in range(4):
                        is_read(dve, st + (q,))
                elif kind == "on":
                    mean_of(4, CW)
                    for t in range(T):
                        sent(v.tensor_scalar(o2[:, t, :], o2[:, t, :], rcol(4, t), None, ALU.mult), on_ready)
                elif kind == "conv":
                    for c in range(2):
                        for h in range(2):
                            is_read(dve, ("ag", c, h, 0))
                    dve.wait_ge(pad_zeroed, 1)
                    uin = upad[:, :, PAD:PAD + S]
                    link(v.tensor_tensor(uin, uin, dw[:, :, :], ALU.mult))
                    for k in range(TAPS):
                        for c in range(CT):
                            src = upad[:, c, k:k + S]
                            if k == 0:
                                ins = v.tensor_scalar(dw[:, c, :], src, convw[:, k, c:c + 1], gcol("conv_b", c),
                                                      ALU.mult, ALU.add)
                            else:
                                ins = v.scalar_tensor_tensor(dw[:, c, :], src, convw[:, k, c:c + 1], dw[:, c, :],
                                                             ALU.mult, ALU.add)
                            sent(ins, conv_ready)
                            if k * CT + c >= CT - 1:
                                dve.wait_ge(conv_ready, k * CT + c - CT + 2)
                elif kind == "cmean":
                    is_full(dve, job)
                    dve.wait_ge(conv_ready, TAPS * CT)
                    freed(v.scalar_tensor_tensor(dw[:, :, :], bcast(pb(job)[:, 0:S], 1, CT), -1.0 / CW, dw[:, :, :],
                                                 ALU.mult, ALU.add), job)
                elif kind == "cvar":
                    is_read(dve, job)
                    link(v.reciprocal(crs, crs))
                    sent(v.tensor_tensor(dw[:, :, :], dw[:, :, :], bcast(crs, 1, CT), ALU.mult), lnorm_ready)
                elif kind == "crms":
                    is_read(dve, job)
                    link(v.reciprocal(crs, crs))
                    for c in range(CT):
                        sent(v.scalar_tensor_tensor(UT[:, 4 + c, :], cz[:, c, :], gcol("conv_out", c), crs, ALU.mult,
                                               ALU.mult), conv_mixed)
                elif kind == "logit":
                    is_full(dve, job)
                    lg = pb(job)[:, 0:T * E].rearrange("p (t e) -> p t e", t=T)
                    link(v.tensor_reduce(aff_[:, 32:34], lg, AX_X, ALU.max, negate=True))
                    a3 = affs_[:, 0:T * E].rearrange("p (t e) -> p t e", t=T)
                    freed(v.tensor_tensor(a3, lg, bcast(aff_[:, 32:34], 2, E), ALU.add), job)
                    dve.wait_ge(logit_exp, 1)
                    link(v.tensor_reduce(aff_[:, 34:36], a3, AX_X, ALU.add))
                    link(v.reciprocal(aff_[:, 36:38], aff_[:, 34:36]))
                    sent(v.tensor_tensor(aff, a3, bcast(aff_[:, 36:38], 2, E), ALU.mult), aff_ready)
                elif kind == "affT":
                    read(job, routew[0:E, :], pb(job)[0:E, 0:S])
                    is_read(dve, job)
                    for r in range(CAP // 8):
                        best = topv[0:E, 8 * r:8 * r + 8]
                        link(v.max(best, routew[0:E, :]))
                        v.max_index(topi[0:E, 8 * r:8 * r + 8], best, routew[0:E, :])
                        link(v.match_replace(routew[0:E, :], best, routew[0:E, :], -1.0))
                    link(v.tensor_copy(topf[0:E, :], topi[0:E, :]))
                    v.tensor_tensor(dgi[0:E, :].rearrange("p (e c) -> p e c", e=E), delta[0:E, :, :],
                                    bcast(topf[0:E, :], 1, E), ALU.mult)
                    for dst, src in ((top4f, topf), (top4g, topv)):
                        ins = v.tensor_copy(dst[0:E, :].rearrange("p (j c) -> p j c", j=FJ), bcast(src[0:E, :], 1, FJ))
                    sent(ins, top_ready)
                elif kind == "spread":
                    is_full(dve, job)
                    for t in range(T):
                        ins = v.tensor_scalar(pick[:, t, :], pb(job)[:, :], tok_part[:, t:t + 1], None, ALU.is_equal)
                    freed(ins, job)
                elif kind == "cols":
                    read(job, ecols_, pb(job)[:, 0:2 * E])
                    is_read(dve, job)

            with dve.Fori(0, E // 2) as it:
                for x in range(2):
                    n_ = it * 2 + (x + 1)
                    e = it * 2 + x
                    dve.wait_ge(gathered, n_)
                    g0 = GAIN_ROWS["norm2"][0]
                    v.tensor_tensor(xsT, bank[5][:, 0:KD * CAP].rearrange("p (k s) -> p k s", k=KD),
                                    bcast(gain[:, g0:g0 + KD], 2, CAP), ALU.mult).then_inc(xs_ready, 1)
                    v.tensor_scalar(spreadT_, tok_free[:, :], ecols[:, 0, bass.ds(e, 1)], ecols[:, 1, bass.ds(e, 1)],
                                    ALU.is_equal, ALU.mult).then_inc(spread_ready, 1)
                    dve.wait_ge(glu_ready, n_)
                    q = x * XCH + 7
                    dve.wait_ge(used[q % SLOTS], it * 3 + q // SLOTS + 1)
                    v.tensor_tensor(hidx, bank[5][:, :], sgx, ALU.mult).then_inc(h_ready, 1)
                    q = x * XCH + XCH - 1
                    dve.wait_ge(used[q % SLOTS], it * 3 + q // SLOTS + 1)
                    v.tensor_copy(eo[:, 1, :], bank[7][:, :]).then_inc(eo1_ready, 1)
            dve.wait_ge(y_done, E)
            for q in range(4):
                sent(v.tensor_copy(SC[:, q // 2, (q % 2) * NB:(q % 2 + 1) * NB], bank[q][:, :]), y_read)
            mean_of(6, D)
            dve.wait_ge(gb2_loaded, 16)
            for t in range(T):
                sent(v.scalar_tensor_tensor(UTf[:, t, :], SC[:, t, :], rcol(6, t), GB[:, :], ALU.mult,
                                       ALU.mult), out_ready)

        @block.tensor
        def _(pe):
            mm = nc.tensor.matmul
            tr = nc.tensor.transpose

            def filled(ins, job):
                ins.then_inc(full[JOB[job] % BANKS], 1)

            def turn_tokens(st):
                for q in range(4):
                    j = st + (q,)
                    bank_taken(pe, j)
                    for kk in range(2):
                        for t in range(T):
                            ins = tr(pb(j)[:, kk * S + t * P:kk * S + (t + 1) * P],
                                     SC[:, t, (2 * q + kk) * P:(2 * q + kk + 1) * P], ident[:, :])
                    filled(ins, j)

            def features_ready(st):
                for q in range(4):
                    is_read(pe, st + (q,))

            def tokens_by_columns(job, lhs, w, n, k_n, stride, off=0):
                bank_taken(pe, job)
                for k in range(k_n):
                    ins = mm(pb(job)[:, 0:n], lhs(k), w[:, k * stride + off:k * stride + off + n],
                             start=(k == 0), stop=(k == k_n - 1))
                filled(ins, job)

            ROTS = [st[1:] for st in STEPS if st[0] == "rot"]
            norm_n = {0: 0, 1: 1, 2: 2, 3: 3}
            for st in STEPS:
                kind = st[0]
                job = st + (0,)
                if kind == "gains":
                    pe.wait_ge(consts_ready, 1)
                    pe.wait_ge(rows_loaded, 16 * 12)
                    filled(tr(pb(job)[:, 0:GAINS], SC[0:GAINS, 0, 0:P], ident[0:GAINS, 0:GAINS]), job)
                    pe.wait_ge(conv_loaded, 16)
                    j, n = ("gains", 1), TAPS * CT
                    filled(tr(pb(j)[:, 0:n], SC[0:n, 0, P:2 * P], ident[0:n, 0:n]), j)
                elif kind == "norm":
                    pe.wait_ge(xn_ready, T * (norm_n[st[1]] + 1))
                    turn_tokens(st)
                    features_ready(st)
                elif kind == "proj":
                    _, c, t = st
                    w, n = slot(("w_in", c)), W_IN_CUTS[c][1]
                    has_weights(pe, ("w_in", c))
                    tokens_by_columns(job, lambda k: UT[:, k, t * P:(t + 1) * P], w, n, KD, n)
                elif kind == "rot":
                    _, c, t = st
                    r = ROTS.index((c, t))
                    bank_taken(pe, job)
                    pe.wait_ge(rot_ready, r + 1)
                    nb = {KV4: 3, KV2: 1}.get(c, 4)
                    for b in range(nb):
                        ins = tr(pb(job)[:, b * P:(b + 1) * P], rot[:, r % 2, b * P:(b + 1) * P], ident[:, :])
                    filled(ins, job)
                elif kind == "cmph":
                    bank_taken(pe, job)
                    pe.wait_ge(blk_ready, 1)
                    has_weights(pe, ("cmp", 0))
                    has_weights(pe, ("cmp", 1))
                    for l in range(LP):
                        for kv in range(2):
                            ins = mm(pb(job)[32 * kv:32 * kv + 32, 0:CH], blk[:, kv, l, :, :].rearrange("p g i -> p (g i)"),
                                     slot(("cmp", kv))[:, l * CH:(l + 1) * CH], start=(l == 0), stop=(l == LP - 1),
                                     skip_group_check=True)
                    filled(ins, job)
                elif kind == "cmpt":
                    bank_taken(pe, job)
                    is_read(pe, ("cmph", 0))
                    for k in range(2):
                        ins = tr(pb(job)[:, k * 64:(k + 1) * 64], hidc[0:64, k * P:(k + 1) * P], ident[0:64, 0:64])
                    filled(ins, job)
                elif kind == "cmpw":
                    bank_taken(pe, job)
                    is_read(pe, ("cmpt", 0))
                    pe.wait_ge(small_loaded, 16 * 5)
                    for g in range(2):
                        for k in range(2):
                            mm(pb(job)[DH * g:DH * (g + 1), 0:16], w2[:, 0, k, :], hidcT[:, k, 16 * g:16 * g + 16],
                               start=(k == 0), stop=(k == 1))
                    for g in range(2):
                        for k in range(2):
                            ins = mm(pb(job)[0:16, DH * (1 + g):DH * (2 + g)], hidcT[:, k, 32 + 16 * g:48 + 16 * g],
                                     w2[:, 1, k, :], start=(k == 0), stop=(k == 1))
                    filled(ins, job)
                elif kind == "S":
                    u = st[1]
                    k, p, t = UNITS[u]
                    need = {"diff": [("rot", c, x, 0) for c in (DQ, DK) for x in range(T)],
                            "cmp": [("rot", NQ, x, 0) for x in range(T)] + [("cmpw", 0)],
                            "sel": [("rot", KV4, x, 0) for x in range(T)],
                            "win": [("rot", KV2, x, 0) for x in range(T)],
                            "grid": [("qk", c, h, 0) for c in range(2) for h in range(2)]}[k]
                    for j in need:
                        is_read(pe, j)
                    tq = slice(t * P, (t + 1) * P)
                    w = key_tiles(u) * P
                    for s in range(2):
                        bank_taken(pe, ("S", u, s))
                    rows = [slice(DH * s, DH * (s + 1)) for s in range(2)]
                    for i in range(4 if k == "cmp" else 2):
                        for s in range(2):
                            j = ("S", u, s)
                            if k == "cmp":
                                ins = mm(pb(j)[:, 16 * i:16 * i + NCB], qkT[rows[s], 8 + i, tq], kcT[rows[s], 0:NCB],
                                         start=True, stop=True)
                                if i == 3:
                                    filled(ins, j)
                                continue
                            b = 2 * p + i
                            if k == "diff":
                                lq, rk = qkT[rows[s], b, tq], qkT[rows[s], 4 + b, 0:w]
                            elif k == "grid":
                                lq, rk = qkT2[rows[s], b, tq], qkT2[rows[s], 4 + b, 0:w]
                            else:
                                lq, rk = qkT[rows[s], 8 + b, tq], qkT[rows[s], 14 if k == "sel" else 15, 0:w]
                            ins = mm(pb(j)[:, S * i:S * i + w], lq, rk, start=True, stop=True)
                            if i == 1:
                                filled(ins, j)
                elif kind == "PT":
                    u = st[1]
                    k, p, t = UNITS[u]
                    sbuf = (probs1 if u < NU1 else probs2)[:, u % 2]
                    for j in range(turns(u)):
                        bank_taken(pe, st + (j,))
                    if k in ("diff", "cmp"):
                        pe.wait_ge(mixed_ready, u + 1)
                    else:
                        pe.wait_ge(exp_ready, u + 1)
                    if k == "cmp":
                        flat = sbuf.rearrange("p m k -> p (m k)")
                        for n in range(8):
                            ins = tr(pb(st + (n // 4,))[0:NCB, (n % 4) * P:(n % 4 + 1) * P], flat[:, 16 * n:16 * n + NCB],
                                     ident[:, :])
                            if n % 4 == 3:
                                filled(ins, st + (n // 4,))
                        continue
                    nk = key_tiles(u)
                    maps = 2 if k == "diff" else 4
                    for m in range(maps):
                        for kk in range(nk):
                            n = m * nk + kk
                            ins = tr(pb(st + (n // 4,))[:, (n % 4) * P:(n % 4 + 1) * P], sbuf[:, m, kk * P:(kk + 1) * P],
                                     ident[:, :])
                            if n % 4 == 3 or n == maps * nk - 1:
                                filled(ins, st + (n // 4,))
                elif kind == "PV":
                    u = st[1]
                    k, p, t = UNITS[u]
                    tb = (turned1 if u < NU1 else turned2)[:, u % 2]
                    bank_taken(pe, job)
                    for j in range(turns(u)):
                        is_read(pe, ("PT", u, j))
                    values = {"diff": [("proj", DV, x, 0) for x in range(T)], "cmp": [("cmpw", 0)],
                              "sel": [("proj", KV4, x, 0) for x in range(T)], "win": [("proj", KV2, x, 0) for x in range(T)],
                              "grid": [("v", x, 0) for x in range(T)]}[k]
                    for j in values:
                        is_read(pe, j)
                    if k == "cmp":
                        for n in range(8):
                            ins = mm(pb(job)[:, n * DH:(n + 1) * DH], tb[0:NCB, n * P:(n + 1) * P],
                                     vcs[0:NCB, DH * (n // 4):DH * (n // 4 + 1)], start=True, stop=True)
                        filled(ins, job)
                        continue
                    nk = key_tiles(u)
                    wd_ = P if k == "diff" else DH
                    for m in range(2 if k == "diff" else 4):
                        for kk in range(nk):
                            if k == "diff":
                                val = vdiff[:, kk, (2 * p + m) * P:(2 * p + m + 1) * P]
                            elif k == "grid":
                                hd = 2 * (2 * p + m % 2) + m // 2
                                val = v2[:, kk, hd * DH:(hd + 1) * DH]
                            else:
                                val = (vsel if k == "sel" else vwin)[:, kk, DH * (m // 2):DH * (m // 2 + 1)]
                            n = m * nk + kk
                            ins = mm(pb(job)[:, m * wd_:(m + 1) * wd_], tb[:, n * P:(n + 1) * P], val,
                                     start=(kk == 0), stop=(kk == nk - 1))
                    filled(ins, job)
                elif kind in ("yaT", "ybT", "oT"):
                    for t in range(T):
                        j = st + (t,)
                        bank_taken(pe, j)
                        if kind == "yaT":
                            pe.wait_ge(ya_ready, 1)
                        elif kind == "ybT":
                            pe.wait_ge(yb_added, 8)
                        else:
                            pe.wait_ge(on_ready, t + 1)
                        src = {"yaT": ya, "ybT": yb, "oT": o2}[kind]
                        for b in range(4):
                            ins = tr(pb(j)[:, b * P:(b + 1) * P], src[:, t, b * P:(b + 1) * P], ident[:, :])
                        filled(ins, j)
                elif kind in ("bra", "brb"):
                    _, t, h = st
                    src = yaT if kind == "bra" else ybT
                    has_weights(pe, (kind,))
                    is_read(pe, ("yaT" if kind == "bra" else "ybT", t))
                    tokens_by_columns(job, lambda k: src[:, k, t * P:(t + 1) * P], slot((kind,)), NB, 4, D, h * NB)
                elif kind == "mT":
                    pe.wait_ge(merged, 4)
                    turn_tokens(st)
                    features_ready(st)
                elif kind in ("wo", "wo2"):
                    _, t, h = st
                    has_weights(pe, (kind, h))
                    if kind == "wo2":
                        is_read(pe, ("oT", 0))
                        is_read(pe, ("oT", 1))
                        pe.wait_ge(conv_mixed, CT)
                    tokens_by_columns(job, lambda k: UT[:, k, t * P:(t + 1) * P], slot((kind, h)), NB, KD, NB)
                elif kind == "gu":
                    _, c, t = st
                    has_weights(pe, ("gu", c))
                    tokens_by_columns(job, lambda k: UT[:, k, t * P:(t + 1) * P], slot(("gu", c)), NB, KD, NB)
                elif kind == "hT":
                    c = st[1]
                    bank_taken(pe, job)
                    for t in range(T):
                        is_read(pe, ("gu", c, t, 0))
                    for kk in range(2):
                        for t in range(T):
                            ins = tr(pb(job)[:, kk * S + t * P:kk * S + (t + 1) * P],
                                     hid[:, (2 * c + t) % 4, kk * P:(kk + 1) * P], ident[:, :])
                    filled(ins, job)
                elif kind == "down":
                    for q in range(4):
                        bank_taken(pe, st + (q,))
                    for k in range(FK):
                        i, kk = k // 4, k % 4
                        if kk == 0:
                            has_weights(pe, ("down", i))
                        if k % 2 == 0:
                            is_read(pe, ("hT", k // 2, 0))
                        for q in range(4):
                            t, h = q // 2, q % 2
                            ins = mm(pb(st + (q,))[:, :], hidT[:, k, t * P:(t + 1) * P],
                                     slot(("down", i))[:, kk * D + h * NB:kk * D + (h + 1) * NB],
                                     start=(k == 0), stop=(k == FK - 1))
                            if k == FK - 1:
                                filled(ins, st + (q,))
                        if kk == 3:
                            ins.then_inc(down_used, 1)
                elif kind in ("qk", "ag"):
                    _, c, h = st
                    ch = ("w_in2", c if kind == "qk" else 3 + c)
                    has_weights(pe, ch)
                    bank_taken(pe, job)
                    for i in range(2):
                        for k in range(KD):
                            ins = mm(pb(job)[:, i * S:(i + 1) * S], slot(ch)[:, k * NB + (2 * h + i) * P:k * NB + (2 * h + i + 1) * P],
                                     UT[:, k, :], start=(k == 0), stop=(k == KD - 1))
                    filled(ins, job)
                elif kind == "v":
                    t = st[1]
                    has_weights(pe, ("w_in2", 2))
                    tokens_by_columns(job, lambda k: UT[:, k, t * P:(t + 1) * P], slot(("w_in2", 2)), NB, KD, NB)
                elif kind in ("cmean", "cvar", "crms"):
                    bank_taken(pe, job)
                    if kind == "cmean":
                        pe.wait_ge(conv_ready, TAPS * CT)
                    else:
                        pe.wait_ge(csq_ready, 1 if kind == "cvar" else 2)
                    src = cz if kind == "cvar" else dw
                    for c in range(CT):
                        ins = mm(pb(job)[:, 0:S], ones[:, :], src[:, c, :], start=(c == 0), stop=(c == CT - 1))
                    filled(ins, job)
                elif kind == "logit":
                    bank_taken(pe, job)
                    for t in range(T):
                        for k in range(KD):
                            ins = mm(pb(job)[:, t * E:(t + 1) * E], UT[:, k, t * P:(t + 1) * P], w_r[:, k, :],
                                     start=(k == 0), stop=(k == KD - 1))
                    filled(ins, job)
                elif kind == "affT":
                    bank_taken(pe, job)
                    pe.wait_ge(aff_ready, 1)
                    for t in range(T):
                        ins = tr(pb(job)[0:E, t * P:(t + 1) * P], aff[:, t, :], ident[:, :])
                    filled(ins, job)
                elif kind == "spread":
                    bank_taken(pe, job)
                    pe.wait_ge(top_ready, 1)
                    filled(mm(pb(job)[:, :], ones[0:E, :], dgi[0:E, :], start=True, stop=True), job)
                elif kind == "cols":
                    bank_taken(pe, job)
                    mm(pb(job)[:, 0:E], top4f[0:E, :], ident[0:E, 0:E], start=True, stop=True)
                    filled(mm(pb(job)[:, E:2 * E], top4g[0:E, :], ident[0:E, 0:E], start=True, stop=True), job)

            last = sorted(JOB, key=JOB.get)[-BANKS:]
            for j in last:
                is_read(pe, j)
            for q in range(4):
                mm(bank[q][:, :], ident[:, :], X[:, q // 2, (q % 2) * NB:(q % 2 + 1) * NB], start=True, stop=False,
                   skip_group_check=True)
            with pe.Fori(0, E // 2) as it:
                for x in range(2):
                    n = it * 2 + (x + 1)
                    e = it * 2 + x

                    def chunk(q):
                        s, o = (x * XCH + q) % SLOTS, (x * XCH + q) // SLOTS
                        pe.wait_ge(loaded[s], it * 48 + (16 * (BASE[s] + o + 1)))
                        return s

                    for k in range(KD):
                        for t in range(T):
                            ins = mm(bank[5][:, k * CAP:(k + 1) * CAP], SC[:, t, k * P:(k + 1) * P],
                                     pick[:, t, bass.ds(e * CAP, CAP)], start=(t == 0), stop=(t == T - 1))
                    ins.then_inc(gathered, 1)
                    pe.wait_ge(xs_ready, n)
                    for q in range(8):
                        s = chunk(q)
                        w = ring[:, s, :].rearrange("p (k f) -> p k f", k=2)
                        for kk in range(2):
                            k = 2 * (q % 4) + kk
                            for j in range(FJ):
                                ins = mm(bank[4 + q // 4][32 * j:32 * j + 32, :], xsT[:, k, :], w[:, kk, j * NB:(j + 1) * NB],
                                         start=(k == 0), stop=(k == KD - 1), tile_position=(0, 32 * j), skip_group_check=True)
                        ins.then_inc(used[s], 1)
                    pe.wait_ge(h_ready, n)
                    for c in range(4):
                        ins = tr(bank[4][:, c * P:(c + 1) * P], hidx[:, c * P:(c + 1) * P], ident[:, :])
                    ins.then_inc(turned_x, 1)
                    pe.wait_ge(hT_ready, n)
                    for c in range(4):
                        s = chunk(8 + c)
                        w = ring[:, s, :].rearrange("p (j f) -> p j f", j=FJ)
                        for h in range(2):
                            for j in range(FJ):
                                ins = mm(bank[6 + h][32 * j:32 * j + 32, :], hidxT[:, c, 32 * j:32 * j + 32],
                                         w[:, j, h * NB:(h + 1) * NB], start=(c == 0), stop=(c == 3),
                                         tile_position=(0, 32 * j), skip_group_check=True)
                        ins.then_inc(used[s], 1)
                    pe.wait_ge(spread_ready, n)
                    pe.wait_ge(eo0_ready, n)
                    pe.wait_ge(eo1_ready, n)
                    for q in range(4):
                        t, h = q // 2, q % 2
                        ins = mm(bank[q][:, :], spreadT_[:, t * P:(t + 1) * P], eo[:, h, :], start=False, stop=False,
                                 skip_group_check=True)
                    ins.then_inc(y_done, 1)


_OUTS = [((1, S, D), "float32")]


def kernel(**inputs):
    import numpy as _np
    import concourse.bacc as _bacc
    from concourse import mybir as _mybir
    from concourse.bass_utils import run_bass_kernel_spmd as _run

    nc = _bacc.Bacc("TRN2", target_bir_lowering=False, num_devices=1)
    arrays, aps = {}, {}
    for name, value in inputs.items():
        a = _np.ascontiguousarray(value)
        arrays[f"in_{name}_dram"] = a
        aps[name] = nc.dram_tensor(f"in_{name}_dram", a.shape, _mybir.dt.from_np(a.dtype), kind="ExternalInput").ap()
    shape, dtype = _OUTS[0]
    out = nc.dram_tensor("out_0_dram", shape, _mybir.dt.from_np(_np.dtype(dtype)), kind="ExternalOutput").ap()
    two_blocks(nc, aps, out)
    r = _run(nc, [arrays], core_ids=[0])
    return r.results[0]["out_0_dram"]
```

```python
import math
from contextlib import ExitStack

import numpy as np

import concourse.bass as bass
from concourse import mybir

ALU = mybir.AluOpType
ACT = mybir.ActivationFunctionType
AX_X = mybir.AxisListType.X
F32 = mybir.dt.float32
F32R = mybir.dt.float32r
I32 = mybir.dt.int32
U32 = mybir.dt.uint32

P = 128
S = 256
T = S // P
D = 1024
KD = D // P
DH = 64
HALF = DH // 2
NB = 512
BANKS = 8
EPS = 1e-6
NEG = -1e30
SCALE = DH ** -0.5
THETA = 10000.0
LAM_INIT = 0.8 - 0.6 * math.exp(0.0)

W_IN_CUTS = [(0, 512), (512, 512), (1024, 512), (1536, 512), (2048, 512), (2560, 280),
             (2840, 512), (3352, 512), (3864, 512), (4376, 512)]
DQ, DK, DV, NQ, KV4, KV2 = range(6)
MG0 = 6
SPLIT_IN = range(1, 5)
CMP_LEN, CMP_STRIDE = 32, 16
NCB = (S - CMP_LEN) // CMP_STRIDE + 1
CH = 256
LP = CMP_LEN // 2
FF = 2816
GU = 256
FC = FF // GU
FK = FF // P

GRID = 64
ROWS = S // GRID
WIN_C = 16
RPB_R, RPB_C = 15, 31
NH2 = 8
CW = 512
CT = CW // P
CV = CT - 1
TAPS = 31
PAD = TAPS // 2
E = 16
CAP = 2 * S // E
EF = 2048
FJ = EF // NB

SLOTS = 8
SLOT = 4096
XCH = 12

GAIN_ROWS = {}
_at = 0
for _name, _n in (("attn", 8), ("ffn", 8), ("norm1", 8), ("norm2", 8), ("attn_out", 4), ("conv_out", 4),
                  ("conv_b", 4), ("ln_g", 4), ("ln_b", 4), ("subln", 1), ("pe_k", 16), ("pe_v", 16)):
    GAIN_ROWS[_name] = (_at, _n)
    _at += _n
GAINS = _at

UNITS1 = ([("diff", p, t) for p in range(2) for t in range(T)] + [("cmp", 0, t) for t in range(T)]
          + [("sel", p, t) for p in range(2) for t in range(T)] + [("win", p, t) for p in range(2) for t in range(T)])
UNITS2 = [("grid", p, t) for p in range(2) for t in range(T)]
UNITS = UNITS1 + UNITS2
NORM_ORDER = [(0, 0), (0, 1), (1, 0), (1, 1), (2, 0), (2, 1), (4, 0), (4, 1), (5, 0), (5, 1), (6, 0), (6, 1)]
NU1 = len(UNITS1)


def key_tiles(u):
    kind, _, t = UNITS[u]
    return T if kind == "grid" else (1 if kind == "cmp" else t + 1)


def turns(u):
    kind = UNITS[u][0]
    if kind == "cmp":
        return 2
    if kind == "diff":
        return 1
    return key_tiles(u)


def expert_slot(n):
    return (5, 3, 1, 4, 6, 7, 2, 0)[n % SLOTS]


def order_of_steps():
    st = [("gains",), ("stats", 0, 0), ("norm", 0, 0), ("stats", 0, 1)]
    lag = []
    for c in range(6):
        for t in range(T):
            if c + 1 in SPLIT_IN and t == 0 and c:
                st.append(("isplit", c + 1, 0))
            if (c, t) == (0, 1):
                st.append(("isplit", 1, 0))
            st.append(("proj", c, t))
            if (c, t) == (0, 0):
                st.append(("norm", 0, 1))
            if c + 1 in SPLIT_IN and t == 1:
                st.append(("isplit", c + 1, 1))
            if c != DV:
                st.append(("rope", c, t))
            if len(lag) > 1:
                st.append(("rot",) + lag.pop(0))
            if c != DV:
                lag.append((c, t))
    fill = {0: [("proj", MG0, 0)],
            1: [("proj", MG0, 1), ("blocks",)],
            2: [("cmph",), ("proj", MG0 + 1, 0), ("cmpt",)],
            3: [("cmpw",), ("proj", MG0 + 1, 1)],
            4: [("proj", MG0 + 2, 0), ("mgs", 0)],
            5: [("proj", MG0 + 2, 1)],
            6: [("yan",), ("proj", MG0 + 3, 0)],
            7: [("yas",), ("proj", MG0 + 3, 1), ("yaT",)],
            8: [("mgs", 1)],
            9: [("bra", 0, 0), ("bra", 1, 0)],
            13: [("bra", 0, 1), ("bra", 1, 1)]}
    st += [("rot",) + x for x in lag] + [("swap",)]
    for i in range(NU1 + 2):
        if i < NU1:
            st.append(("S", i))
        st += fill.get(i, [])
        if 1 <= i <= NU1:
            st.append(("PT", i - 1))
        if i >= 2:
            st.append(("PV", i - 2))
    st += [("ybT", t) for t in range(T)] + [("brb", t, h) for t in range(T) for h in range(2)]
    st += [("mT", 0), ("wo", 0, 0), ("mT", 1), ("wo", 0, 1), ("stats", 1, 0), ("split", 0, 0), ("wo", 1, 0), ("norm", 1, 0)]
    st += [("split", 0, 1), ("wo", 1, 1), ("stats", 1, 1), ("gu_first",), ("norm", 1, 1), ("gu", 0, 0), ("split", 1, 0),
           ("gu", 0, 1), ("split", 1, 1)]
    for c in range(1, FC - 1):
        st += [("split", c + 1, 0), ("gu", c, 0), ("gu", c, 1), ("split", c + 1, 1), ("hT", c - 1)]
    st += [("gu", FC - 1, 0), ("dsplit", 0), ("gu", FC - 1, 1), ("dsplit", 1), ("hT", FC - 2)]
    for n in range(FK // 2 - 2):
        st += [("dn", n), ("dsplit", n + 2)] + ([("hT", FC - 1)] if n == 0 else [])
    st += [("dn", 9), ("stats", 2, 0), ("dn", 10), ("dn", 11), ("norm", 2, 0), ("stats", 2, 1), ("v", 0), ("norm", 2, 1)]
    st += [("ag", c, h) for c in range(2) for h in range(2)] + [("conv",)]
    st += [("qk", 0, 0), ("cpe",), ("qk", 1, 0), ("qk", 0, 1)]
    before = {1: [("qk", 1, 1), ("cmean",)], 2: [("v", 1), ("crms",)]}
    fill = {1: [("cvar",)], 3: [("wo2c", 0, 0), ("wo2c", 0, 1), ("wo2c", 1, 0)], 4: [("wo2c", 1, 1)]}
    n2 = len(UNITS2)
    for i in range(n2 + 2):
        if i < n2:
            st.append(("S", NU1 + i))
        st += before.get(i, [])
        if 1 <= i <= n2:
            st.append(("PT", NU1 + i - 1))
        if i >= 2:
            st.append(("PV", NU1 + i - 2))
        st += fill.get(i, [])
    st += [("on",)] + [("oT", t) for t in range(T)]
    st += [("wo2", 0, 0), ("wo2", 0, 1), ("stats", 3, 0), ("wo2", 1, 0), ("norm", 3, 0), ("wo2", 1, 1)]
    st += [("stats", 3, 1), ("logit", 0), ("norm", 3, 1), ("soft", 0), ("logit", 1), ("soft", 1), ("affT",), ("spread",), ("cols",)]
    return st


def jobs_of(step):
    kind = step[0]
    n = {"gains": 2, "norm": 2, "yaT": T, "mT": 2, "stats": 0, "rope": 0, "split": 0, "gu_first": 0, "dsplit": 0, "isplit": 0, "S": 2, "blocks": 0, "swap": 0, "yan": 0, "yas": 0,
         "mgs": 0, "on": 0, "conv": 0, "soft": 0}.get(kind, 1)
    if kind == "PT":
        n = turns(step[1])
    if kind == "dn":
        return [("down", t, h) for t in range(T) for h in range(2)] if step[1] == 0 else []
    return [step + (i,) for i in range(n)]


def two_blocks(nc, A, out):
    STEPS = order_of_steps()
    FIRST = -sum(len(jobs_of(st)) for st in STEPS) % BANKS
    JOB = {}
    for st in STEPS:
        for j in jobs_of(st):
            JOB[j] = FIRST + len(JOB)

    def turn(job):
        return JOB[job] // BANKS + (1 if JOB[job] % BANKS >= FIRST else 0)

    CHUNKS = ([("w_in", c) for c in range(6)] + [("cmp", 0), ("cmp", 1)] + [("w_in", c) for c in range(MG0, 10)]
              + [("bra",), ("brb",), ("wo", 0), ("wo", 1)])
    SLOT_OF = dict(zip(CHUNKS, [4, 0, 1, 2, 4, 0, 1, 2, 4, 3, 0, 1, 2, 3, 4, 0]))
    late = ([("gu", c) for c in range(FC)] + [("down", i) for i in range(6)] + [("w_in2", c) for c in (2, 3, 4, 0, 1)]
            + [("wo2", 0), ("wo2", 1)])
    late_slots = [(3, 4, 0, 5)[c % 4] for c in range(FC)] + [5, 3, 4, 0, 5, 3] + [4, 0, 5, 3, 1] + [2, 0]
    SLOT_OF.update(dict(zip(late, late_slots)))
    CHUNKS += late
    LAST_USE = {("cmp", 0): ("cmph", 0), ("cmp", 1): ("cmph", 0), ("bra",): ("bra", 1, 1, 0), ("brb",): ("brb", 1, 1, 0)}
    for c in range(10):
        LAST_USE[("w_in", c)] = ("proj", c, 1, 0)
    for h in range(2):
        LAST_USE[("wo", h)] = ("wo", 1, h, 0)
        LAST_USE[("wo2", h)] = ("wo2", T - 1, h, 0)
        LAST_USE[("w_in2", h)] = ("qk", h, 1, 0)
        LAST_USE[("w_in2", 3 + h)] = ("ag", h, 1, 0)
    LAST_USE[("w_in2", 2)] = ("v", 1, 0)
    for c in range(FC):
        LAST_USE[("gu", c)] = ("gu", c, 1, 0)
    LAST_USE[("down", 5)] = ("down", 1, 1)

    with ExitStack() as ctx:
        def sb(name, *shape, dt=F32):
            return ctx.enter_context(nc.sbuf_tensor(name, list(shape), dt))

        def sem(name):
            return ctx.enter_context(nc.semaphore(name))

        bank = [ctx.enter_context(nc.psum_tensor(f"bank{b}", [P, NB], F32)) for b in range(BANKS)]

        ring_at = (nc.sbuf_base + 31) // 32 * 32
        ring = sb("ring", P, SLOTS, SLOT)
        wsplit = nc.alloc_sbuf_tensor_at("wsplit", [P, 2, 2, KD // 2 * NB], F32R, offset=ring_at + 4 * SLOT)
        usplit = nc.alloc_sbuf_tensor_at("usplit", [P, 2, KD, S], F32R, offset=ring_at + 7 * 4 * SLOT)
        hsplit = nc.alloc_sbuf_tensor_at("hsplit", [P, 2, 2, 2, S], F32R, offset=ring_at + 7 * 4 * SLOT + 2 * SLOT)
        isplit = [nc.alloc_sbuf_tensor_at("isplit0", [P, 2, KD // 2 * NB], F32R, offset=ring_at + 6 * 4 * SLOT)]
        ixsplit = nc.alloc_sbuf_tensor_at("ixsplit", [P, 2, KD, S], F32R, offset=ring_at + 3 * 4 * SLOT)
        ident = sb("ident", P, P)
        ones = sb("ones", P, P)
        causal = sb("causal", P, S)
        cmp_add = sb("cmp_add", P, T, 16)
        cmp_keep = sb("cmp_keep", P, T, 16)
        delta = sb("delta", E, E, CAP)
        tok_free = sb("tok_free", P, S)
        tok_int = sb("tok_int", P, S, dt=I32)
        part_int = sb("part_int", P, T, dt=I32)
        tok_part = sb("tok_part", P, T)
        inv_freq = sb("inv_freq", P, HALF)
        pos_int = sb("pos_int", P, T, dt=I32)
        pos = sb("pos", P, T)
        trig = sb("trig", P, 3, T, HALF)
        ang = sb("ang", P, T * HALF)
        angk = sb("angk", P, T * HALF)
        gain = sb("gain", P, 96)
        convw = sb("convw", P, TAPS, CT)
        subln = sb("subln", P, 1)
        ystat = sb("ystat", P, 16)
        mhalf = sb("mhalf", P, 8)
        eps_col = sb("eps_col", P, 1)
        w_r = sb("w_r", P, KD, E)
        w2 = sb("w2", P, 2, 2, DH)
        dl = sb("dl", P, 4, DH)
        dlp = sb("dlp", P, 2, DH)
        lamv = sb("lamv", P, 8)
        stat = sb("stat", P, 64)
        pair = sb("pair", P, T, 4)
        nmax = sb("nmax", P, len(UNITS), 8)
        rsum = sb("rsum", P, len(UNITS), 8)
        rinv = sb("rinv", P, len(UNITS), 8)
        kcT = sb("kcT", P, 16)
        vcs = sb("vcs", P, 2 * DH)
        rpbp = sb("rpbp", P, P)
        X = sb("X", P, T, D)
        UT = sb("UT", P, KD, S)
        SC = sb("SC", P, T, D)
        GB = sb("GB", P, D)
        ARENA = 9200
        PROBS_AT = 2 * T * P + T * 24 + CH + 2 * DH
        arena_at = (nc.sbuf_base + 31) // 32 * 32
        arena = sb("arena", P, ARENA)
        isplit.append(nc.alloc_sbuf_tensor_at("isplit1", [P, 2, KD // 2 * NB], F32R, offset=arena_at + 4 * PROBS_AT))

        def carve(base, sizes):
            views, at = [], 0
            for n in sizes:
                views.append(base[:, at:at + n])
                at += n
            assert at <= base.shape[1], (at, base.shape)
            return views

        vsel, vwin, ngate, hidc, hidcT, probs_, turned_, ya_, yb_, kswap = carve(
            arena, [T * P, T * P, T * 24, CH, 2 * DH, 2 * 1024, 2 * 1024, T * NB, T * NB, 2 * S])
        over = ring[:, 5:8, :].rearrange("p a b -> p (a b)")
        qkT, mg, yaT, ybT, vdiff, blk = carve(over, [16 * S, T * 2 * D, 4 * S, 4 * S, T * NB, 2 * LP * 32])
        qkT = qkT.rearrange("p (b s) -> p b s", s=S)
        mg = mg.rearrange("p (t c) -> p t c", t=T)
        yaT = yaT.rearrange("p (b s) -> p b s", s=S)
        ybT = ybT.rearrange("p (b s) -> p b s", s=S)
        vdiff = vdiff.rearrange("p (t c) -> p t c", t=T)
        blk = blk.rearrange("p (v l g i) -> p v l g i", v=2, l=LP, g=2)
        vsel = vsel.rearrange("p (t c) -> p t c", t=T)
        vwin = vwin.rearrange("p (t c) -> p t c", t=T)
        ngate = ngate.rearrange("p (t b h) -> p t b h", t=T, b=3)
        hidcT = hidcT.rearrange("p (k c) -> p k c", k=2)
        kswap = kswap.rearrange("p (v s) -> p v s", v=2)
        ya = ya_.rearrange("p (t c) -> p t c", t=T)
        yb = yb_.rearrange("p (t c) -> p t c", t=T)
        UTf = UT[:, :, :].rearrange("p k s -> p (k s)").rearrange("p (t d) -> p t d", t=T)
        scf = SC[:, :, :].rearrange("p t c -> p (t c)")
        rope_a, rope_b = scf[:, 0:NB], scf[:, NB:2 * NB]
        rot = scf[:, 2 * NB:4 * NB].rearrange("p (b c) -> p b c", b=2)
        sgate = scf[:, 0:2 * GU].rearrange("p (b c) -> p b c", b=2)
        hid = scf[:, 2 * GU:6 * GU].rearrange("p (b c) -> p b c", b=4)
        hidT = arena[:, 0:FK * S].rearrange("p (k s) -> p k s", s=S)
        probs2_, qkT2_, v2_ = carve(arena, [2 * 1024, 8 * S, T * NB])
        bias = arena[:, ARENA - 3072:ARENA].rearrange("p (h d c) -> p h d c", h=NH2, d=6)
        qkT2 = qkT2_.rearrange("p (b s) -> p b s", s=S)
        v2 = v2_.rearrange("p (t c) -> p t c", t=T)
        o2 = GB[:, :].rearrange("p (t c) -> p t c", t=T)
        upad_, dw_, cz_, sg2_ = carve(ring[:, 7, :], [CT * (S + 2 * PAD), CT * S, CT * S, 904])
        upad = upad_.rearrange("p (c s) -> p c s", c=CT)
        dw = dw_.rearrange("p (c s) -> p c s", c=CT)
        cz = cz_.rearrange("p (c s) -> p c s", c=CT)
        crs = sg2_[:, 0:S]
        diag = ring[:, 6, 0:TAPS * P].rearrange("p (k c) -> p k c", k=TAPS)
        probs1 = probs_.rearrange("p (b m k) -> p b m k", b=2, m=4)
        turned1 = turned_.rearrange("p (b n) -> p b n", b=2)
        probs2 = probs2_.rearrange("p (b m k) -> p b m k", b=2, m=4)
        turned2 = scf.rearrange("p (b n) -> p b n", b=2)
        (pick_, pick_e_, xs_, xsT_, sgx, hidx, hidxT_, eo_, spreadT_, routew, topv, topf, top4f, top4g, dgi, dgg, topi_, ecols_, affs_,
         aff_) = carve(arena, [T * E * CAP, T * CAP, D // 4, KD * CAP, NB, NB, NB, 2 * NB, S, S, CAP, CAP, P, P, NB, 0, CAP, 2 * E, 64, 64])
        pick = pick_.rearrange("p (t n) -> p t n", t=T)
        pick_e = pick_e_.rearrange("p (t n) -> p t n", t=T)
        xsT = xsT_.rearrange("p (k s) -> p k s", s=CAP)
        hidxT = hidxT_.rearrange("p (c n) -> p c n", c=4)
        eo = eo_.rearrange("p (h n) -> p h n", h=2)
        ecols = ecols_.rearrange("p (v e) -> p v e", v=2)
        aff = aff_[:, 0:T * E].rearrange("p (t e) -> p t e", t=T)
        topi = topi_.bitcast(U32)

        full = [sem(f"bank_full{b}") for b in range(BANKS)]
        free = [sem(f"bank_free{b}") for b in range(BANKS)]
        loaded = [sem(f"slot_loaded{s}") for s in range(SLOTS)]
        used = [sem(f"slot_used{s}") for s in range(SLOTS)]
        x_loaded, rows_loaded, conv_loaded = sem("x_loaded"), sem("rows_loaded"), sem("conv_loaded")
        pos_loaded = sem("pos_loaded")
        small_loaded, gb_loaded, gb2_loaded = sem("small_loaded"), sem("gb_loaded"), sem("gb2_loaded")
        rpb_loaded, rpb_stored, bias_loaded = sem("rpb_loaded"), sem("rpb_stored"), sem("bias_loaded")
        swapped = sem("swapped")
        pstep, vstep, astep = sem("pool_step"), sem("vector_step"), sem("scalar_step")
        consts_ready, bias_ready = sem("consts_ready"), sem("bias_ready")
        blk_zeroed, pad_zeroed = sem("blk_zeroed"), sem("pad_zeroed")
        angle_ready, trig_ready = sem("angle_ready"), sem("trig_ready")
        lam_dot, lam_exp = sem("lam_dot"), sem("lam_exp")
        squares, mean_sq, rstd_ready, xn_ready = sem("squares"), sem("mean_sq"), sem("rstd_ready"), sem("xn_ready")
        rot_ready, blk_ready = sem("rot_ready"), sem("blk_ready")
        max_ready, exp_ready, mixed_ready = sem("max_ready"), sem("exp_ready"), sem("mixed_ready")
        gate_ready, mg_ready, ya_ready, merged = sem("gate_ready"), sem("mg_ready"), sem("ya_ready"), sem("merged")
        uh_ready, ul_ready, wh_ready, wl_ready = sem("uh_ready"), sem("ul_ready"), sem("wh_ready"), sem("wl_ready")
        ihalf_used, ih_ready, il_ready = sem("ihalf_used"), sem("ih_ready"), sem("il_ready")
        ixh_ready, ixl_ready = sem("ixh_ready"), sem("ixl_ready")
        half_used, down_used = sem("half_used"), sem("down_used")
        dh_ready, dl_ready = sem("dh_ready"), sem("dl_ready")
        sg_ready = sem("sg_ready")
        conv_ready, csq_ready = sem("conv_ready"), sem("csq_ready")
        lnorm_ready, silu_ready, conv_mixed = sem("lnorm_ready"), sem("silu_ready"), sem("conv_mixed")
        diag_ready, u_ready = sem("diag_ready"), sem("u_ready")
        on_ready, xg_ready, yb_added = sem("on_ready"), sem("xg_ready"), sem("yb_added")
        ya_mean, ya_rstd = sem("ya_mean"), sem("ya_rstd")
        logit_exp, aff_ready, top_ready, pick_ready = (sem("logit_exp"), sem("aff_ready"),
                                                                 sem("top_ready"), sem("pick_ready"))
        pick_e_ready, xs_copied, xs_turned = sem("pick_e_ready"), sem("xs_copied"), sem("xs_turned")
        gathered, xs_ready, glu_ready, h_ready = sem("gathered"), sem("xs_ready"), sem("glu_ready"), sem("h_ready")
        turned_x, hT_ready, eo0_ready, eo1_ready, spread_ready = (sem("turned_x"), sem("hT_ready"), sem("eo0_ready"),
                                                                  sem("eo1_ready"), sem("spread_ready"))
        y_done, out_ready, stored = sem("y_done"), sem("out_ready"), sem("stored")

        def pb(job):
            return bank[JOB[job] % BANKS]

        def is_full(eng, job):
            eng.wait_ge(full[JOB[job] % BANKS], turn(job))

        def is_read(eng, job):
            eng.wait_ge(free[JOB[job] % BANKS], turn(job))

        def bank_taken(eng, job):
            if turn(job) > 1:
                eng.wait_ge(free[JOB[job] % BANKS], turn(job) - 1)

        def slot(ch):
            return ring[:, SLOT_OF[ch], :]

        def bcast(ap, dim, n):
            shape = list(ap.shape)
            shape.insert(dim, n)
            return ap.unsqueeze(dim).broadcast_to(shape)

        def gcol(name, k=0):
            return gain[:, GAIN_ROWS[name][0] + k:GAIN_ROWS[name][0] + k + 1]

        class Sent:

            def __init__(self, eng):
                self.eng, self.count, self.last = eng, {}, None

            def __call__(self, ins, sem_):
                key = id(sem_)
                self.count[key] = self.count.get(key, 0) + 1
                self.last = (sem_, self.count[key])
                ins.then_inc(sem_, 1)

            def bank(self, ins, job):
                b = JOB[job] % BANKS
                self.last = (free[b], turn(job))
                ins.then_inc(free[b], 1)

            def own(self):
                if self.last:
                    self.eng.wait_ge(*self.last)

        RPB = nc.dram_tensor("rpb_rows", (NH2 * 7, GRID, P), F32).ap()

        def kt(ap):
            return ap.rearrange("(k p) n -> p k n", p=P)

        def source(ch):
            kind, s = ch[0], slot(ch)
            if kind == "w_in":
                c0, n = W_IN_CUTS[ch[1]]
                return [(s[:, 0:KD * n].rearrange("p (k n) -> p k n", k=KD), kt(A["w_in"][0])[:, :, c0:c0 + n])]
            if kind == "cmp":
                w = A[("cmp_k_w1", "cmp_v_w1")[ch[1]]][0]
                return [(s.rearrange("p (k n) -> p k n", k=LP), kt(w))]
            if kind in ("bra", "brb"):
                w = A["w_branch_a" if kind == "bra" else "w_branch_b"][0]
                return [(s.rearrange("p (k n) -> p k n", k=4), kt(w))]
            if kind in ("wo", "wo2", "w_in2"):
                w = A[{"wo": "w_out", "wo2": "w_out_2", "w_in2": "w_in_2"}[kind]][0]
                return [(s.rearrange("p (k n) -> p k n", k=KD), kt(w)[:, :, ch[1] * NB:(ch[1] + 1) * NB])]
            if kind == "gu":
                d = s.rearrange("p (k v n) -> p k v n", k=KD, v=2)
                return [(d[:, :, v, :], kt(A[w][0])[:, :, ch[1] * GU:(ch[1] + 1) * GU])
                        for v, w in enumerate(("w_gate", "w_up"))]
            n = min(4, FK - 4 * ch[1])
            return [(s[:, 0:n * D].rearrange("p (k n) -> p k n", k=n),
                     kt(A["w_down"][0])[:, 4 * ch[1]:4 * ch[1] + n, :])]

        block = ctx.enter_context(nc.Block())

        LOADS = {}
        tot = [0] * SLOTS
        for ch in CHUNKS:
            tot[SLOT_OF[ch]] += 2 if ch[0] == "gu" else 1
            LOADS[ch] = tot[SLOT_OF[ch]]
        BASE = list(tot)

        def has_weights(eng, ch):
            eng.wait_ge(loaded[SLOT_OF[ch]], 16 * LOADS[ch])

        @block.sync
        def _(sp):
            sp.dma_start(X[:, :, :], A["x"][0].rearrange("(t p) d -> p t d", p=P)).then_inc(x_loaded, 16)
            sp.wait_ge(rows_loaded, 16 * 12)
            owner = {}
            for ch in CHUNKS:
                s = SLOT_OF[ch]
                if s in owner:
                    prev = owner[s]
                    if ch in (("w_in2", 1), ("wo2", 0)):
                        is_full(sp, ("down", 1, 1))
                    elif prev[0] == "w_in" and prev[1] in SPLIT_IN:
                        sp.wait_ge(il_ready, 2 * prev[1])
                    elif prev[0] == "gu":
                        sp.wait_ge(wl_ready, 2 * prev[1] + 2)
                    elif prev[0] == "down":
                        sp.wait_ge(dl_ready, min(2 * prev[1] + 2, FK // 2))
                    else:
                        is_full(sp, LAST_USE[prev])
                elif ch == ("w_in", MG0 + 1):
                    is_full(sp, ("proj", MG0 - 1, 1, 0))
                elif s >= 5:
                    is_read(sp, ("wo", 1, 1, 0))
                owner[s] = ch
                for dst, src in source(ch):
                    sp.dma_start(dst, src).then_inc(loaded[s], 16)
                if ch == ("gu", 4):
                    is_read(sp, ("wo", 1, 1, 0))
                    sp.wait_ge(rpb_stored, 16)
                    for q in range(2):
                        for h in range(NH2):
                            src = bass.AP(tensor=RPB.tensor, offset=(h * 7 + 1 - q) * GRID * P + GRID - 1,
                                          ap=[[P - 1, GRID], [GRID * P, 6], [1, GRID]])
                            sp.dma_start(bias[GRID * q:GRID * (q + 1), h, :, :], src).then_inc(bias_loaded, 16)

            wg = A["w_gate_2"][0].rearrange("e (k p) f -> e p k f", p=P)
            wu = A["w_up_2"][0].rearrange("e (k p) f -> e p k f", p=P)
            wd = A["w_down_2"][0].rearrange("e (k p) f -> e p k f", p=P)

            def load_expert(e, q, s):
                if q < 8:
                    w = wg if q < 4 else wu
                    src = w[e, :, 2 * (q % 4):2 * (q % 4) + 2, :].rearrange("o p k f -> (o p) k f")
                    dst = ring[:, s, :].rearrange("p (k f) -> p k f", k=2)
                else:
                    h, c0 = (q - 8) // 2, 8 * (q % 2)
                    src = wd[e, :, c0:c0 + 8, h * NB:(h + 1) * NB].rearrange("o p k f -> (o p) k f")
                    dst = ring[:, s, :].rearrange("p (k f) -> p k f", k=8)
                sp.dma_start(dst, src).then_inc(loaded[s], 16)

            for n in range(2 * XCH):
                s, o = expert_slot(n), n // SLOTS
                if o:
                    sp.wait_ge(used[s], o)
                elif s >= 6:
                    sp.wait_ge(conv_mixed, CT)
                else:
                    is_full(sp, LAST_USE[owner[s]])
                load_expert(slice(n // XCH, n // XCH + 1), n % XCH, s)
            with sp.Fori(1, E // 2) as it:
                for n in range(2 * XCH):
                    s, o = expert_slot(n), n // SLOTS
                    sp.wait_ge(used[s], it * 3 + o)
                    if n < XCH:
                        load_expert(bass.ds(it * 2, 1), n % XCH, s)
                    else:
                        load_expert(bass.ds(it * 2 + 1, 1), n % XCH, s)
            for q in range(2 * T):
                t, cols = q // 2, slice(q % 2 * NB, (q % 2 + 1) * NB)
                sp.wait_ge(out_ready, q + 1)
                sp.dma_start(out[0].rearrange("(t p) d -> p t d", p=P)[:, t, cols], UTf[:, t, cols]).then_inc(stored, 16)
            sp.wait_ge(stored, 16 * 2 * T)


        @block.gpsimd
        def _(pool):
            g = nc.gpsimd
            sent = Sent(pool)

            def link(ins):
                sent(ins, pstep)
                sent.own()

            for i in range(HALF):
                g.memset(inv_freq[:, i:i + 1], float(np.float32(1.0) / np.float32(THETA ** (2 * i / DH))))
            g.memset(ones[:, :], 1.0)
            g.memset(mhalf[:, :], -0.5)
            g.memset(eps_col[:, :], EPS)
            g.memset(ident[:, :], 0.0)
            g.memset(causal[:, :], 0.0)
            g.memset(cmp_add[:, :, :], 0.0)
            g.memset(cmp_keep[:, :, :], 1.0)
            g.memset(delta[:, :, :], 1.0)
            g.memset(rpbp[:, :], 0.0)
            g.iota(tok_int[:, :], [[1, S]], base=0, channel_multiplier=0)
            link(g.iota(part_int[:, :], [[P, T]], base=0, channel_multiplier=1))
            g.affine_select(out=ident[:, :], in_=ident[:, :], compare_op=ALU.not_equal, fill=1.0, base=0,
                            pattern=[[-1, P]], channel_multiplier=1)
            g.affine_select(out=causal[:, P:S], in_=causal[:, P:S], compare_op=ALU.is_ge, fill=NEG, base=0,
                            pattern=[[-1, P]], channel_multiplier=1)
            for m, fill in ((cmp_add, NEG), (cmp_keep, 0.0)):
                g.affine_select(out=m[:, :, :], in_=m[:, :, :], compare_op=ALU.is_ge, fill=fill, base=1 - CMP_LEN,
                                pattern=[[P, T], [-CMP_STRIDE, 16]], channel_multiplier=1)
            sent(g.affine_select(out=delta[:, :, :], in_=delta[:, :, :], compare_op=ALU.is_equal, fill=0.0, base=0,
                            pattern=[[1, E], [0, CAP]], channel_multiplier=-1), consts_ready)
            sent(g.memset(blk[:, :, :, :, :], 0.0), blk_zeroed)

            def power(k, out_, in_, ready, done, count, w):
                sent.own()
                pool.wait_ge(ready, count)
                sent(g.tensor_tensor(out_, in_, mhalf[:, 0:w], ALU.pow), done)

            def rstd(k):
                i, t = NORM_ORDER[k]
                if i == 2:
                    power(i, pair[:, t, 2:4], pair[:, t, 0:2], mean_sq, rstd_ready, k + 1, 2)
                    return
                power(i, stat[:, 8 * i + 4 + t:8 * i + 5 + t], stat[:, 8 * i + 2 + t:8 * i + 3 + t], mean_sq, rstd_ready, k + 1, 1)

            pool.wait_ge(consts_ready, 1)
            rstd(0)
            rstd(1)
            power(0, ystat[:, 8:16], ystat[:, 0:8], ya_mean, ya_rstd, 1, 8)
            rstd(2)
            rstd(3)
            is_full(pool, ("gu", FC - 1, 1, 0))
            g.memset(upad[:, :, 0:PAD], 0.0)
            sent(g.memset(upad[:, :, PAD + S:], 0.0), pad_zeroed)
            pool.wait_ge(bias_loaded, 16 * 2 * NH2)
            for q in range(2):
                b = bias[GRID * q:GRID * (q + 1), :, :, :].rearrange("p h d c -> p (h d) c")
                sent.own()
                hi = b[:, :, 0:GRID - WIN_C]
                lo = b[:, :, WIN_C:GRID]
                link(g.affine_select(out=hi, in_=hi, compare_op=ALU.is_ge, fill=NEG, base=WIN_C // 2,
                                     pattern=[[0, 6 * NH2], [1, GRID - WIN_C]], channel_multiplier=-1))
                last = g.affine_select(out=lo, in_=lo, compare_op=ALU.is_ge, fill=NEG, base=WIN_C // 2 - 1 - WIN_C,
                                       pattern=[[0, 6 * NH2], [-1, GRID - WIN_C]], channel_multiplier=1)
                sent(last, bias_ready)
            for k in range(4, len(NORM_ORDER)):
                rstd(k)

        @block.scalar
        def _(act):
            a = nc.scalar
            sent = Sent(act)

            r0 = 0
            for name in ("attn_norm_g", "ffn_norm_g", "norm1_g_2", "norm2_g_2", "attn_out_g_2", "conv_out_g_2",
                         "conv_b_2", "conv_ln_g_2", "conv_ln_b_2", "diff_subln_g"):
                w = A[name][0].rearrange("(r c) -> r c", c=P)
                act.dma_start(UTf[r0:r0 + w.shape[0], 0, 0:P], w).then_inc(rows_loaded, 16)
                r0 += w.shape[0]
            for name in ("cmp_pe_k", "cmp_pe_v"):
                act.dma_start(UTf[r0:r0 + LP, 0, 0:P], A[name][0].rearrange("(r l) d -> r (l d)", l=2)).then_inc(rows_loaded, 16)
                r0 += LP
            act.dma_start(UTf[0:TAPS * CT, 0, P:2 * P], A["conv_w_2"][0].rearrange("k (c n) -> (k c) n", n=P)).then_inc(conv_loaded, 16)
            act.dma_start(pos_int[:, :], A["positions"].rearrange("a (t p) -> p (a t)", p=P),
                          allow_slow_non_contiguous=True).then_inc(pos_loaded, 16)
            act.dma_start(dl[:, :, :], A["diff_lambda"][0].rearrange("(o r) d -> o r d", o=1).broadcast_to([P, 4, DH])).then_inc(pos_loaded, 16)

            def later_loads():
                act.dma_start(w_r[:, :, :], kt(A["w_router_2"][0])).then_inc(small_loaded, 16)
                for v, name in enumerate(("cmp_k_w2", "cmp_v_w2")):
                    act.dma_start(w2[:, v, :, :], kt(A[name][0])).then_inc(small_loaded, 16)
                act.dma_start(GB[:, :], A["final_norm_g"].rearrange("(o d) -> o d", o=1).broadcast_to([P, D])).then_inc(gb_loaded, 16)
                act.wait_ge(consts_ready, 1)
                for h in range(NH2):
                    act.dma_start(rpbp[7 * h:7 * h + 7, GRID - WIN_C:GRID - WIN_C + RPB_C],
                                  A["rpb_2"][0][h, RPB_R // 2 - 3:RPB_R // 2 + 4, :]).then_inc(rpb_loaded, 16)

            def squares_of(i, t, src, junk):
                if i == 0 and t == 0:
                    act.wait_ge(x_loaded, 16)
                if i in (1, 5):
                    for h in range(2):
                        is_read(act, ("wo" if i == 1 else "wo2", t, h, 0))
                if i == 4:
                    for p_ in range(2):
                        is_read(act, ("PV", NU1 + 2 * p_ + t, 0))
                sent(a.activation(junk, src[:, t, :], ACT.Square,
                                  accum_out=stat[:, 8 * i + t:8 * i + t + 1]), squares)

            def read(job, out_, in_, f=ACT.Copy, **kw):
                is_full(act, job)
                sent.bank(a.activation(out_, in_, f, **kw), job)

            for st in STEPS:
                kind = st[0]
                sent.own()
                job = st + (0,)
                if kind == "stats":
                    k, t = st[1:]
                    i = {0: 0, 1: 1, 2: 2, 3: 5}[k]
                    if i == 2:
                        for h in range(2):
                            is_read(act, ("down", t, h))
                        junk = UT[:, :, t * P:(t + 1) * P]
                        fold = lambda x: x.rearrange("p (k c) -> p k c", k=KD)
                        sent(a.activation(junk, fold(X[:, t, :]), ACT.Square, accum_out=stat[:, 16 + t:17 + t]), astep)
                        sent.own()
                        act.wait_ge(xg_ready, t + 1)
                        sent(a.activation(junk, fold(SC[:, t, :]), ACT.Square, accum_out=stat[:, 24 + t:25 + t]), squares)
                    else:
                        squares_of(i, t, X, SC[:, t, :])
                    if i == 0 and t == 1:
                        act.wait_ge(angle_ready, 1)
                        sent(a.activation(trig[:, 0:2, :, :], trig[:, 0:2, :, :], ACT.Sin), trig_ready)
                        act.wait_ge(lam_dot, 1)
                        sent(a.activation(lamv[:, 2:4], lamv[:, 0:2], ACT.Exp), lam_exp)
                        later_loads()
                elif kind == "proj":
                    _, c, t = st
                    if c == DV:
                        read(job, vdiff[:, t, :], pb(job)[:, :])
                    elif c >= MG0:
                        read(job, mg[:, t, (c - MG0) * NB:(c - MG0 + 1) * NB], pb(job)[:, :])
                elif kind == "rot":
                    _, c, t = st
                    b0, nb = {DQ: (0, 4), DK: (4, 4), NQ: (8, 4), KV4: (12, 3), KV2: (15, 1)}[c]
                    read(job, qkT[:, b0:b0 + nb, t * P:(t + 1) * P],
                         pb(job)[:, 0:nb * P].rearrange("p (b s) -> p b s", b=nb))
                elif kind == "swap":
                    for t in range(T):
                        is_read(act, ("rot", KV4, t, 0))
                    for g_ in range(2):
                        act.dma_start(kswap[DH * (1 - g_):DH * (2 - g_), :, :],
                                      qkT[DH * g_:DH * (g_ + 1), 12:14, :]).then_inc(swapped, 16)
                    for t in range(T):
                        is_read(act, ("proj", KV2, t, 0))
                    sent(a.activation(ngate[:, :, :, :], ngate[:, :, :, :], ACT.Sigmoid), gate_ready)
                    act.wait_ge(rpb_loaded, 16 * NH2)
                    act.dma_start(RPB, bcast(rpbp[0:7 * NH2, :], 1, GRID)).then_inc(rpb_stored, 16)
                elif kind == "cmph":
                    read(job, hidc[0:64, :], pb(job)[0:64, 0:CH], ACT.Silu)
                elif kind == "cmpt":
                    read(job, hidcT[:, :, 0:64], pb(job)[:, 0:2 * 64].rearrange("p (k c) -> p k c", k=2))
                elif kind == "S":
                    u = st[1]
                    k, _, t = UNITS[u]
                    sbuf = (probs1 if u < NU1 else probs2)[:, u % 2]
                    act.wait_ge(max_ready, u + 1)
                    if k == "cmp":
                        v = sbuf.rearrange("p m k -> p (m k)")[:, 0:8 * 16].rearrange("p (n i) -> p n i", n=8)
                        sent(a.activation(v[:, :, 0:NCB], v[:, :, 0:NCB], ACT.Exp), exp_ready)
                    else:
                        w = key_tiles(u) * P
                        for m in range(4):
                            ins = a.activation(sbuf[:, m, 0:w], sbuf[:, m, 0:w], ACT.Exp, bias=nmax[:, u, m:m + 1],
                                               accum_out=rsum[:, u, m:m + 1])
                        sent(ins, exp_ready)
                elif kind == "PT":
                    u = st[1]
                    k, _, t = UNITS[u]
                    tb = (turned1 if u < NU1 else turned2)[:, u % 2]
                    if u >= 2:
                        is_full(act, ("PV", u - 2, 0))
                    rows = NCB if k == "cmp" else P
                    cols = (2 if k == "diff" else 4) * key_tiles(u) * P // turns(u) if k != "cmp" else NB
                    for j in range(turns(u)):
                        read(st + (j,), tb[0:rows, j * NB:j * NB + cols], pb(st + (j,))[0:rows, 0:cols])
                elif kind == "mgs":
                    b = st[1]
                    for c in range(2):
                        for t in range(T):
                            is_read(act, ("proj", MG0 + 2 * b + c, t, 0))
                    half = mg[:, :, b * D:(b + 1) * D]
                    sent(a.activation(half, half, ACT.Sigmoid), mg_ready)
                elif kind in ("yaT", "ybT"):
                    dst = yaT if kind == "yaT" else ybT
                    for t in (range(T) if kind == "yaT" else st[1:]):
                        j = ("yaT", t) if kind == "yaT" else job
                        read(j, dst[:, :, t * P:(t + 1) * P], pb(j)[:, :].rearrange("p (b s) -> p b s", b=4),
                             scale=subln[:, 0:1] if kind == "yaT" else 1.0)
                elif kind == "mT":
                    t = st[1]
                    for q in range(2):
                        j = st + (q,)
                        read(j, UT[:, 4 * q:4 * q + 4, t * P:(t + 1) * P], pb(j)[:, :].rearrange("p (b s) -> p b s", b=4))
                elif kind == "norm" and st[1] in (0, 1):
                    t = st[2]
                    xs, done = (ixsplit, ixh_ready) if st[1] == 0 else (usplit, uh_ready)
                    for q in range(2):
                        is_read(act, st + (q,))
                        tk = slice(t * P, (t + 1) * P)
                        sent(a.activation(xs[:, 0, 4 * q:4 * q + 4, tk], UT[:, 4 * q:4 * q + 4, tk], ACT.Copy), done)
                elif kind == "isplit":
                    _, c, h = st
                    has_weights(act, ("w_in", c))
                    if c > 1:
                        if h == 0:
                            act.wait_ge(ihalf_used, c - 1)
                        else:
                            is_full(act, ("proj", c - 1, 1, 0))
                    half = slot(("w_in", c))[:, h * (SLOT // 2):(h + 1) * (SLOT // 2)]
                    sent(a.activation(isplit[h][:, 0, :], half, ACT.Copy), ih_ready)
                elif kind == "split":
                    _, c, h = st
                    has_weights(act, ("gu", c))
                    if c == 0:
                        is_full(act, LAST_USE[("w_in", 9)] if h == 0 else LAST_USE[("bra",)])
                    elif h == 0:
                        act.wait_ge(half_used, c)
                    else:
                        is_full(act, ("gu", c - 1, 1, 0))
                    half = slot(("gu", c))[:, h * (SLOT // 2):(h + 1) * (SLOT // 2)]
                    sent(a.activation(wsplit[:, h, 0, :], half, ACT.Copy), wh_ready)
                elif kind == "dsplit":
                    n = st[1]
                    b = n % 2
                    has_weights(act, ("down", n // 2))
                    if n == 0:
                        act.wait_ge(half_used, FC)
                    elif n >= 2:
                        act.wait_ge(down_used, n - 1)
                    else:
                        is_full(act, ("gu", FC - 1, 1, 0))
                    half = slot(("down", n // 2))[:, b * (SLOT // 2):(b + 1) * (SLOT // 2)]
                    for i in range(2):
                        cols = slice(i * SLOT // 4, (i + 1) * SLOT // 4)
                        sent(a.activation(wsplit[:, b, 0, cols], half[:, cols], ACT.Copy), dh_ready)
                    if n == 0:
                        is_full(act, ("gu", FC - 1, 1, 0))
                    is_read(act, ("hT", n, 0))
                    sent(a.activation(hsplit[:, b, 0, :, :], hidT[:, 2 * n:2 * n + 2, :], ACT.Copy), dh_ready)
                elif kind == "gu":
                    n = 2 * st[1] + st[2]
                    is_full(act, job)
                    if n >= 2:
                        is_read(act, ("gu", (n - 2) // 2, n % 2, 0))
                    sent(a.activation(sgate[:, n % 2], pb(job)[:, 0:GU], ACT.Silu), sg_ready)
                    for tap in range(2 * n, min(2 * n + 2, TAPS)):
                        sent(a.activation(diag[:, tap, :], ident[:, :], ACT.Copy, scale=convw[:, tap, CT - 1:CT]), diag_ready)
                elif kind == "hT":
                    c = st[1]
                    read(job, hidT[:, 2 * c:2 * c + 2, :].rearrange("p k s -> p (k s)"), pb(job)[:, :])
                elif kind == "qk":
                    _, c, h = st
                    read(job, qkT2[:, 4 * c + 2 * h:4 * c + 2 * h + 2, :].rearrange("p k s -> p (k s)"), pb(job)[:, :])
                elif kind == "v":
                    read(job, v2[:, st[1], :], pb(job)[:, :])
                elif kind == "ag":
                    _, c, h = st
                    src = pb(job)[:, :].rearrange("p (k s) -> p k s", k=2)
                    if c == 0:
                        read(job, upad[:, 2 * h:2 * h + 2, PAD:PAD + S], src)
                    else:
                        read(job, dw[:, 2 * h:2 * h + 2, :], src, ACT.Sigmoid)
                elif kind == "cpe":
                    read(job, dw[:, CT - 1, :], pb(job)[:, 0:S], ACT.Identity, bias=gcol("conv_b", CT - 1))
                elif kind == "on":
                    for t in range(T):
                        squares_of(4, t, o2, SC[:, t, 0:NB])
                        sent.own()
                elif kind == "oT":
                    t = st[1]
                    is_full(act, job)
                    for k in range(4):
                        ins = a.activation(UT[:, k, t * P:(t + 1) * P], pb(job)[:, k * P:(k + 1) * P], ACT.Copy,
                                           scale=gcol("attn_out", k))
                    sent.bank(ins, job)
                    if t < T - 1:
                        continue
                    act.dma_start(GB[:, :], A["final_g_2"].rearrange("(o d) -> o d", o=1).broadcast_to([P, D])).then_inc(gb2_loaded, 16)
                elif kind == "cvar":
                    is_read(act, ("cmean", 0))
                    sent(a.activation(cz[:, :, :], dw[:, :, :], ACT.Square), csq_ready)
                    read(job, crs, pb(job)[:, 0:S], ACT.Sqrt, bias=eps_col[:, 0:1], scale=1.0 / CW)
                    act.wait_ge(lnorm_ready, 1)
                    for c in range(CT):
                        sent(a.activation(cz[:, c, :], dw[:, c, :], ACT.Silu, bias=gcol("ln_b", c),
                                     scale=gcol("ln_g", c)), silu_ready)
                elif kind == "crms":
                    act.wait_ge(silu_ready, CT)
                    sent(a.activation(dw[:, :, :], cz[:, :, :], ACT.Square), csq_ready)
                    read(job, crs, pb(job)[:, 0:S], ACT.Sqrt, bias=eps_col[:, 0:1], scale=1.0 / CW)
                elif kind == "soft":
                    t = st[1]
                    is_read(act, ("logit", t, 0))
                    sent(a.activation(affs_[:, t * E:(t + 1) * E], affs_[:, t * E:(t + 1) * E], ACT.Exp), logit_exp)

            with act.Fori(0, E // 2) as it:
                for x in range(2):
                    n = it * 2 + (x + 1)
                    q = x * XCH + 3
                    act.wait_ge(used[expert_slot(q)], it * 3 + q // SLOTS + 1)
                    a.activation(sgx, bank[4][:, :], ACT.Silu).then_inc(glu_ready, 1)
                    act.wait_ge(turned_x, n)
                    a.activation(hidxT_, bank[4][:, :], ACT.Copy).then_inc(hT_ready, 1)
                    q = x * XCH + 9
                    act.wait_ge(used[expert_slot(q)], it * 3 + q // SLOTS + 1)
                    a.activation(eo[:, 0, :], bank[6][:, :], ACT.Copy).then_inc(eo0_ready, 1)
            for h in range(2):
                for t in range(T):
                    act.wait_ge(y_done, 2 * T * (E - 1) + T * h + t + 1)
                    ins = a.activation(SC[:, t, h * NB:(h + 1) * NB], bank[2 * t + h][:, :], ACT.Square,
                                       accum_out=stat[:, 56 + 2 * t + h:57 + 2 * t + h])
                    if h == 1:
                        sent(ins, squares)

        @block.vector
        def _(dve):
            v = nc.vector
            sent = Sent(dve)
            freed = sent.bank

            def link(ins):
                sent(ins, vstep)
                sent.own()

            def read(job, out_, in_):
                is_full(dve, job)
                freed(v.tensor_copy(out_, in_), job)

            def features(job, t, q, name):
                is_full(dve, job)
                g0 = GAIN_ROWS[name][0] + 4 * q
                freed(v.tensor_tensor(UT[:, 4 * q:4 * q + 4, t * P:(t + 1) * P], pb(job)[:, :].rearrange("p (b s) -> p b s", b=4),
                                      bcast(gain[:, g0:g0 + 4], 2, P), ALU.mult), job)

            def mean_of(i, t, width):
                k = NORM_ORDER.index((i, t))
                dve.wait_ge(squares, k + 1)
                sent(v.tensor_scalar(stat[:, 8 * i + 2 + t:8 * i + 3 + t], stat[:, 8 * i + t:8 * i + t + 1], 1.0 / width, EPS,
                                     ALU.mult, ALU.add), mean_sq)
                dve.wait_ge(rstd_ready, k + 1)

            def rcol(i, t):
                return stat[:, 8 * i + 4 + t:8 * i + 5 + t]

            def angles():
                dve.wait_ge(pos_loaded, 16 * 2)
                dve.wait_ge(consts_ready, 1)
                v.tensor_copy(tok_free[:, :], tok_int[:, :])
                v.tensor_copy(tok_part[:, :], part_int[:, :])
                link(v.tensor_copy(pos[:, :], pos_int[:, :]))
                for t in range(T):
                    ins = v.tensor_scalar(ang[:, t * HALF:(t + 1) * HALF], inv_freq[:, :], pos[:, t:t + 1], None, ALU.mult)
                link(ins)
                big = 1.5 * 2.0 ** 23
                two_pi = [6.28125, float(np.float32(0.00193500518798828125)), 0.0]
                two_pi[2] = 2 * math.pi - two_pi[0] - two_pi[1]
                link(v.tensor_scalar(angk[:, :], ang[:, :], 1 / (2 * math.pi), big, ALU.mult, ALU.add))
                link(v.tensor_scalar(angk[:, :], angk[:, :], big, None, ALU.subtract))
                for c in two_pi:
                    link(v.scalar_tensor_tensor(ang[:, :], angk[:, :], -c, ang[:, :], ALU.mult, ALU.add))
                lim = 3.1415925
                s_ = trig[:, 0, :, :].rearrange("p t i -> p (t i)")
                c_ = trig[:, 1, :, :].rearrange("p t i -> p (t i)")
                link(v.tensor_scalar(ang[:, :], ang[:, :], 0.0, None, ALU.add))
                v.tensor_scalar(s_, ang[:, :], lim, -lim, ALU.min, ALU.max)
                link(v.tensor_scalar(angk[:, :], ang[:, :], math.pi / 2, -2 * math.pi, ALU.is_gt, ALU.mult))
                link(v.scalar_tensor_tensor(ang[:, :], ang[:, :], math.pi / 2, angk[:, :], ALU.add, ALU.add))
                sent(v.tensor_scalar(c_, ang[:, :], lim, -lim, ALU.min, ALU.max), angle_ready)

            def lam():
                d2 = dl[:, :, :].rearrange("p (a b) d -> p a b d", b=2)
                link(v.tensor_tensor(dlp[:, :, :], d2[:, :, 0, :], d2[:, :, 1, :], ALU.mult))
                sent(v.tensor_reduce(lamv[:, 0:2], dlp[:, :, :], AX_X, ALU.add), lam_dot)

            def neg_lam():
                dve.wait_ge(lam_exp, 1)
                link(v.tensor_tensor(lamv[:, 4:5], lamv[:, 3:4], lamv[:, 2:3], ALU.subtract))
                link(v.tensor_scalar(lamv[:, 5:6], lamv[:, 4:5], -LAM_INIT, None, ALU.add))
                dve.wait_ge(trig_ready, 1)
                link(v.tensor_scalar(trig[:, 2, :, :], trig[:, 0, :, :], -1.0, None, ALU.mult))

            def rope(src, dst, t, heads, off):
                a3 = rope_a[:, off:off + heads * DH].rearrange("p (n r) -> p n r", r=HALF)
                x3 = src.rearrange("p (n r) -> p n r", r=HALF)
                v.tensor_tensor(a3, x3, bcast(trig[:, 1, t, :], 1, 2 * heads), ALU.mult)
                b4 = rope_b[:, off:off + heads * DH].rearrange("p (n h r) -> p n h r", h=2, r=HALF)
                x4 = src.rearrange("p (n h r) -> p n h r", h=2, r=HALF)
                v.tensor_tensor(b4[:, :, 0, :], x4[:, :, 1, :], bcast(trig[:, 2, t, :], 1, heads), ALU.mult)
                return v.tensor_tensor(b4[:, :, 1, :], x4[:, :, 0, :], bcast(trig[:, 0, t, :], 1, heads), ALU.mult)

            ROTS = [st[1:] for st in STEPS if st[0] == "rot"]

            def softmax_scale(u, k):
                link(v.reciprocal(rinv[:, u, 0:k], rsum[:, u, 0:k]))

            def scores(u):
                kind, p, t = UNITS[u]
                sbuf = (probs1 if u < NU1 else probs2)[:, u % 2]
                if u >= 2:
                    is_full(dve, ("PT", u - 2, turns(u - 2) - 1))
                if kind == "cmp":
                    sv = sbuf.rearrange("p m k -> p (m k)")[:, 0:8 * 16].rearrange("p (n i) -> p n i", n=8)
                    for s in range(2):
                        job = ("S", u, s)
                        is_full(dve, job)
                        freed(v.scalar_tensor_tensor(
                            sv[:, 4 * s:4 * s + 4, 0:NCB], pb(job)[:, 0:64].rearrange("p (n i) -> p n i", n=4)[:, :, 0:NCB],
                            SCALE, bcast(cmp_add[:, t, 0:NCB], 1, 4), ALU.mult, ALU.add), job)
                    is_read(dve, ("S", u, 0))
                    is_read(dve, ("S", u, 1))
                    link(v.tensor_reduce(nmax[:, u, 0:8], sv[:, :, 0:NCB], AX_X, ALU.max, negate=True))
                    sent(v.tensor_tensor(sv[:, :, 0:NCB], sv[:, :, 0:NCB], bcast(nmax[:, u, 0:8], 2, NCB),
                                    ALU.add), max_ready)
                    return
                w = key_tiles(u) * P
                if kind == "grid":
                    dve.wait_ge(bias_ready, 2)
                for s in range(2):
                    job = ("S", u, s)
                    if kind == "grid":
                        m = bias.rearrange("p h d c -> p h (d c)")[:, 4 * p + s:4 * p + s + 3:2, (2 - 2 * t) * GRID:(6 - 2 * t) * GRID]
                    else:
                        m = bcast(causal[:, S - w:S], 1, 2)
                    is_full(dve, job)
                    freed(v.scalar_tensor_tensor(
                        sbuf[:, 2 * s:2 * s + 2, 0:w], pb(job)[:, :].rearrange("p (m k) -> p m k", m=2)[:, :, 0:w],
                        SCALE, m, ALU.mult, ALU.add), job)
                is_read(dve, ("S", u, 0))
                is_read(dve, ("S", u, 1))
                sent(v.tensor_reduce(nmax[:, u, 0:4], sbuf[:, :, 0:w], AX_X, ALU.max, negate=True), max_ready)

            def after_exp(u):
                kind, p, t = UNITS[u]
                sbuf = probs1[:, u % 2]
                if kind == "diff":
                    dve.wait_ge(exp_ready, u + 1)
                    w = key_tiles(u) * P
                    softmax_scale(u, 4)
                    link(v.tensor_scalar(rinv[:, u, 2:4], rinv[:, u, 2:4], lamv[:, 5:6], None, ALU.mult))
                    for i in range(2):
                        ins = v.tensor_scalar(sbuf[:, 2 + i, 0:w], sbuf[:, 2 + i, 0:w], rinv[:, u, 2 + i:3 + i], None, ALU.mult)
                    link(ins)
                    for i in range(2):
                        ins = v.scalar_tensor_tensor(sbuf[:, i, 0:w], sbuf[:, i, 0:w], rinv[:, u, i:i + 1],
                                                     sbuf[:, 2 + i, 0:w], ALU.mult, ALU.add)
                    sent(ins, mixed_ready)
                elif kind == "cmp":
                    dve.wait_ge(exp_ready, u + 1)
                    sv = sbuf.rearrange("p m k -> p (m k)")[:, 0:8 * 16].rearrange("p (n i) -> p n i", n=8)
                    v.tensor_reduce(rsum[:, u, 0:8], sv[:, :, 0:NCB], AX_X, ALU.add)
                    sent(v.tensor_tensor(sv[:, :, 0:NCB], sv[:, :, 0:NCB], bcast(cmp_keep[:, t, 0:NCB], 1, 8),
                                    ALU.mult), mixed_ready)
                    dve.wait_ge(mixed_ready, u + 1)

            added = [0]

            def outputs(u):
                kind, p, t = UNITS[u]
                job = ("PV", u, 0)
                if kind == "diff":
                    read(job, ya[:, t, 2 * P * p:2 * P * (p + 1)], pb(job)[:, 0:2 * P])
                    return
                dve.wait_ge(exp_ready, u + 1)
                if kind == "cmp":
                    dve.wait_ge(gate_ready, 1)
                    softmax_scale(u, 8)
                    link(v.tensor_tensor(rinv[:, u, :], rinv[:, u, :], ngate[:, t, 0, :], ALU.mult))
                    is_full(dve, job)
                    freed(v.tensor_tensor(yb[:, t, :].rearrange("p (n r) -> p n r", n=8),
                                          pb(job)[:, :].rearrange("p (n r) -> p n r", n=8),
                                          bcast(rinv[:, u, :], 2, DH), ALU.mult), job)
                    is_read(dve, job)
                    return
                softmax_scale(u, 4)
                o3 = pb(job)[:, 0:4 * DH].rearrange("p (m r) -> p m r", m=4)
                if kind == "grid":
                    is_full(dve, job)
                    dst = o2[:, t, :].rearrange("p (b s r) -> p s b r", s=2, r=DH)[:, :, 2 * p:2 * p + 2, :]
                    freed(v.tensor_tensor(dst, o3.rearrange("p (s i) r -> p s i r", s=2),
                                          bcast(rinv[:, u, 0:4], 2, DH).rearrange("p (s i) r -> p s i r", s=2), ALU.mult), job)
                    return
                br = 1 if kind == "sel" else 2
                gt = ngate[:, t, br, :].rearrange("p (g b) -> p g b", g=2)[:, :, 2 * p:2 * p + 2]
                r2 = rinv[:, u, 0:4].rearrange("p (g b) -> p g b", g=2)
                link(v.tensor_tensor(r2, r2, gt, ALU.mult))
                tmp = scf[:, 0:4 * DH].rearrange("p (m r) -> p m r", m=4)
                is_full(dve, job)
                freed(v.tensor_tensor(tmp, o3, bcast(rinv[:, u, 0:4], 2, DH), ALU.mult), job)
                is_read(dve, job)
                dst = yb[:, t, :].rearrange("p (g b r) -> p g b r", g=2, r=DH)[:, :, 2 * p:2 * p + 2, :]
                sent(v.tensor_tensor(dst, dst, tmp.rearrange("p (g b) r -> p g b r", g=2), ALU.add), yb_added)
                added[0] += 1
                dve.wait_ge(yb_added, added[0])

            for st in STEPS:
                kind = st[0]
                sent.own()
                job = st + (0,)
                if kind == "gains":
                    read(("gains", 0), gain[:, 0:GAINS], pb(("gains", 0))[:, 0:GAINS])
                    read(("gains", 1), convw[:, :, :].rearrange("p k c -> p (k c)"), pb(("gains", 1))[:, 0:TAPS * CT])
                    is_read(dve, ("gains", 0))
                    is_read(dve, ("gains", 1))
                elif kind == "stats" and st[1] == 2:
                    t = st[2]
                    dve.wait_ge(gb_loaded, 16)
                    sent(v.tensor_tensor(SC[:, t, :], X[:, t, :], GB[:, :], ALU.mult), xg_ready)
                    k = NORM_ORDER.index((2, t))
                    dve.wait_ge(squares, k + 1)
                    v.tensor_scalar(stat[:, 26 + t:27 + t], stat[:, 24 + t:25 + t], 1.0 / D, None, ALU.mult)
                    link(v.tensor_scalar(pair[:, t, 0:1], stat[:, 16 + t:17 + t], 1.0 / D, EPS, ALU.mult, ALU.add))
                    sent(v.scalar_tensor_tensor(pair[:, t, 1:2], pair[:, t, 0:1], EPS, stat[:, 26 + t:27 + t], ALU.mult, ALU.add),
                         mean_sq)
                    dve.wait_ge(rstd_ready, k + 1)
                    v.tensor_scalar(X[:, t, :], SC[:, t, :], pair[:, t, 2:3], None, ALU.mult)
                    sent.own()
                    sent(v.tensor_scalar(SC[:, t, :], SC[:, t, :], pair[:, t, 3:4], None, ALU.mult), xn_ready)
                elif kind == "stats":
                    k, t = st[1:]
                    i = {0: 0, 1: 1, 3: 5}[k]
                    if (k, t) == (0, 1):
                        angles()
                        lam()
                        sent.own()
                    mean_of(i, t, D)
                    sent(v.tensor_scalar(SC[:, t, :], X[:, t, :], rcol(i, t), None, ALU.mult), xn_ready)
                elif kind == "norm":
                    k, t = st[1:]
                    for q in range(2):
                        features(st + (q,), t, q, ("attn", "ffn", "norm1", "norm2")[k])
                    if k in (0, 1):
                        xs, half_done, done = (ixsplit, ixh_ready, ixl_ready) if k == 0 else (usplit, uh_ready, ul_ready)
                        for q in range(2):
                            dve.wait_ge(half_done, 2 * t + q + 1)
                            tk = slice(t * P, (t + 1) * P)
                            sent(v.tensor_tensor(xs[:, 1, 4 * q:4 * q + 4, tk], UT[:, 4 * q:4 * q + 4, tk],
                                                 xs[:, 0, 4 * q:4 * q + 4, tk], ALU.subtract), done)
                    if k == 0 and t == 1:
                        neg_lam()
                        link(v.tensor_scalar(subln[:, :], gcol("subln"), 1.0 - LAM_INIT, None, ALU.mult))
                elif kind == "rope":
                    _, c, t = st
                    job = ("proj", c, t, 0)
                    r = ROTS.index((c, t))
                    buf = rot[:, r % 2]
                    is_full(dve, job)
                    if r < 2:
                        is_full(dve, ("norm", 0, 1, 1))
                    else:
                        is_full(dve, ("rot",) + ROTS[r - 2] + (0,))
                    if c in (DQ, DK, NQ):
                        link(rope(pb(job)[:, :], buf, t, 8, 0))
                        if c == NQ:
                            o = buf.rearrange("p (b g r) -> p g b r", g=2, r=DH)
                            x1, x2 = (z.rearrange("p (g b r) -> p g b r", g=2, r=DH) for z in (rope_a, rope_b))
                            sent(v.tensor_tensor(o, x1, x2, ALU.add), rot_ready)
                        else:
                            sent(v.tensor_tensor(buf, rope_a, rope_b, ALU.add), rot_ready)
                        freed(v.tensor_copy(lamv[:, 6:7], pb(job)[:, 0:1]), job)
                    elif c == KV4:
                        rope(pb(job)[:, 0:P], buf, t, 2, 0)
                        rope(pb(job)[:, 2 * P:3 * P], buf, t, 2, 2 * P)
                        v.tensor_copy(buf[:, P:2 * P], pb(job)[:, P:2 * P])
                        freed(v.tensor_copy(vsel[:, t, :], pb(job)[:, 3 * P:4 * P]), job)
                        is_read(dve, job)
                        o, x1, x2 = (z.rearrange("p (a b) -> p a b", b=2 * P)[:, :, 0:P] for z in (buf, rope_a, rope_b))
                        sent(v.tensor_tensor(o, x1, x2, ALU.add), rot_ready)
                    else:
                        rope(pb(job)[:, 0:P], buf, t, 2, 0)
                        v.tensor_copy(vwin[:, t, :], pb(job)[:, P:2 * P])
                        freed(v.tensor_copy(ngate[:, t, :, :].rearrange("p b h -> p (b h)"), pb(job)[:, 2 * P:2 * P + 24]), job)
                        is_read(dve, job)
                        sent(v.tensor_tensor(buf[:, 0:P], rope_a[:, 0:P], rope_b[:, 0:P], ALU.add), rot_ready)
                elif kind == "blocks":
                    dve.wait_ge(swapped, 32)
                    dve.wait_ge(blk_zeroed, 1)
                    for t in range(T):
                        is_read(dve, ("rot", KV4, t, 0))
                    for kv in range(2):
                        pe0 = GAIN_ROWS[("pe_k", "pe_v")[kv]][0]
                        for hf in range(2):
                            for g in range(2):
                                src = (qkT[:, 12 + kv, :] if g == hf else kswap[:, kv, :])[DH * hf:DH * hf + DH, :]
                                win = bass.AP(tensor=src.tensor, offset=src.offset + hf,
                                              ap=[list(src.ap[0]), [2, LP], [CMP_STRIDE, NCB]])
                                pe_ = bcast(gain[DH * hf:DH * hf + DH, pe0:pe0 + LP], 2, NCB)
                                ins = v.tensor_tensor(blk[DH * hf:DH * hf + DH, kv, :, g, 0:NCB], win, pe_, ALU.add)
                    sent(ins, blk_ready)
                elif kind == "cmpw":
                    is_full(dve, job)
                    v.tensor_copy(kcT[:, :], pb(job)[:, 0:16])
                    freed(v.tensor_copy(vcs[0:16, :], pb(job)[0:16, 64:64 + 2 * DH]), job)
                elif kind == "S":
                    scores(st[1])
                elif kind == "PT":
                    if st[1] < NU1:
                        after_exp(st[1])
                elif kind == "PV":
                    outputs(st[1])
                elif kind == "yan":
                    for u in range(4):
                        is_read(dve, ("PV", u, 0))
                    sq = scf[:, 0:D]
                    link(v.tensor_tensor(sq, ya_, ya_, ALU.mult))
                    link(v.tensor_reduce(ystat[:, 0:8], sq.rearrange("p (n r) -> p n r", n=8), AX_X, ALU.add))
                    sent(v.tensor_scalar(ystat[:, 0:8], ystat[:, 0:8], 1.0 / P, EPS, ALU.mult, ALU.add), ya_mean)
                elif kind == "yas":
                    dve.wait_ge(ya_rstd, 1)
                    y3 = ya_.rearrange("p (n r) -> p n r", n=8)
                    sent(v.tensor_tensor(y3, y3, bcast(ystat[:, 8:16], 2, P), ALU.mult), ya_ready)
                elif kind == "bra":
                    _, t, h = st
                    m = mg[:, t, h * NB:(h + 1) * NB]
                    dve.wait_ge(mg_ready, 1)
                    is_full(dve, job)
                    freed(v.tensor_tensor(m, pb(job)[:, :], m, ALU.mult), job)
                elif kind == "brb":
                    _, t, h = st
                    o = SC[:, t, h * NB:(h + 1) * NB]
                    dve.wait_ge(mg_ready, 2)
                    is_full(dve, job)
                    freed(v.tensor_tensor(o, pb(job)[:, :], mg[:, t, D + h * NB:D + (h + 1) * NB], ALU.mult), job)
                    is_read(dve, job)
                    is_read(dve, ("bra", t, h, 0))
                    sent(v.tensor_tensor(o, o, mg[:, t, h * NB:(h + 1) * NB], ALU.add), merged)
                elif kind in ("wo", "wo2c", "wo2"):
                    _, t, h = st
                    o = X[:, t, h * NB:(h + 1) * NB]
                    is_full(dve, job)
                    freed(v.tensor_tensor(o, pb(job)[:, :], o, ALU.add), job)
                elif kind == "split":
                    _, c, h = st
                    dve.wait_ge(wh_ready, 2 * c + h + 1)
                    half = slot(("gu", c))[:, h * (SLOT // 2):(h + 1) * (SLOT // 2)]
                    sent(v.tensor_tensor(wsplit[:, h, 1, :], half, wsplit[:, h, 0, :], ALU.subtract), wl_ready)
                elif kind == "isplit":
                    _, c, h = st
                    dve.wait_ge(ih_ready, 2 * c - 1 + h)
                    half = slot(("w_in", c))[:, h * (SLOT // 2):(h + 1) * (SLOT // 2)]
                    sent(v.tensor_tensor(isplit[h][:, 1, :], half, isplit[h][:, 0, :], ALU.subtract), il_ready)
                elif kind == "dsplit":
                    n = st[1]
                    b = n % 2
                    half = slot(("down", n // 2))[:, b * (SLOT // 2):(b + 1) * (SLOT // 2)]
                    for i in range(2):
                        cols = slice(i * SLOT // 4, (i + 1) * SLOT // 4)
                        dve.wait_ge(dh_ready, 3 * n + 1 + i)
                        v.tensor_tensor(wsplit[:, b, 1, cols], half[:, cols], wsplit[:, b, 0, cols], ALU.subtract)
                    dve.wait_ge(dh_ready, 3 * n + 3)
                    sent(v.tensor_tensor(hsplit[:, b, 1, :, :], hidT[:, 2 * n:2 * n + 2, :], hsplit[:, b, 0, :, :], ALU.subtract),
                         dl_ready)
                elif kind == "gu":
                    _, c, t = st
                    k = 2 * c + t
                    dve.wait_ge(sg_ready, k + 1)
                    if c >= 2:
                        is_full(dve, ("hT", c - 2, 0))
                    freed(v.tensor_tensor(hid[:, k % 4], pb(job)[:, GU:2 * GU], sgate[:, k % 2], ALU.mult), job)
                elif kind == "dn" and st[1] in (9, 11):
                    t = (st[1] - 9) // 2
                    for h in range(2):
                        j = ("down", t, h)
                        o = X[:, t, h * NB:(h + 1) * NB]
                        is_full(dve, j)
                        freed(v.tensor_tensor(o, pb(j)[:, :], o, ALU.add), j)
                elif kind == "on":
                    for t in range(T):
                        mean_of(4, t, CW)
                        sent(v.tensor_scalar(o2[:, t, :], o2[:, t, :], rcol(4, t), None, ALU.mult), on_ready)
                elif kind == "conv":
                    for c in range(2):
                        for h in range(2):
                            is_read(dve, ("ag", c, h, 0))
                    dve.wait_ge(pad_zeroed, 1)
                    uin = upad[:, :, PAD:PAD + S]
                    sent(v.tensor_tensor(uin, uin, dw[:, :, :], ALU.mult), u_ready)
                    sent.own()
                    for k in range(TAPS):
                        for c in range(CV):
                            src = upad[:, c, k:k + S]
                            if k == 0:
                                ins = v.tensor_scalar(dw[:, c, :], src, convw[:, k, c:c + 1], gcol("conv_b", c),
                                                      ALU.mult, ALU.add)
                            else:
                                ins = v.scalar_tensor_tensor(dw[:, c, :], src, convw[:, k, c:c + 1], dw[:, c, :],
                                                             ALU.mult, ALU.add)
                            sent(ins, conv_ready)
                            if k * CV + c >= CV - 1:
                                dve.wait_ge(conv_ready, k * CV + c - CV + 2)
                elif kind == "cmean":
                    is_full(dve, job)
                    dve.wait_ge(conv_ready, TAPS * CV)
                    is_read(dve, ("cpe", 0))
                    freed(v.scalar_tensor_tensor(dw[:, :, :], bcast(pb(job)[:, 0:S], 1, CT), -1.0 / CW, dw[:, :, :],
                                                 ALU.mult, ALU.add), job)
                elif kind == "cvar":
                    is_read(dve, job)
                    link(v.reciprocal(crs, crs))
                    sent(v.tensor_tensor(dw[:, :, :], dw[:, :, :], bcast(crs, 1, CT), ALU.mult), lnorm_ready)
                elif kind == "crms":
                    is_read(dve, job)
                    link(v.reciprocal(crs, crs))
                    for c in range(CT):
                        sent(v.scalar_tensor_tensor(UT[:, 4 + c, :], cz[:, c, :], gcol("conv_out", c), crs, ALU.mult,
                                               ALU.mult), conv_mixed)
                elif kind == "soft":
                    job = ("logit", st[1], 0)
                    is_full(dve, job)
                    t = st[1]
                    lg, a_ = pb(job)[:, 0:E], affs_[:, t * E:(t + 1) * E]
                    link(v.tensor_reduce(aff_[:, 32 + t:33 + t], lg, AX_X, ALU.max, negate=True))
                    freed(v.tensor_scalar(a_, lg, aff_[:, 32 + t:33 + t], None, ALU.add), job)
                    dve.wait_ge(logit_exp, t + 1)
                    link(v.tensor_reduce(aff_[:, 34 + t:35 + t], a_, AX_X, ALU.add))
                    link(v.reciprocal(aff_[:, 36 + t:37 + t], aff_[:, 34 + t:35 + t]))
                    sent(v.tensor_scalar(aff[:, t, :], a_, aff_[:, 36 + t:37 + t], None, ALU.mult), aff_ready)
                elif kind == "affT":
                    read(job, routew[0:E, :], pb(job)[0:E, 0:S])
                    is_read(dve, job)
                    for r in range(CAP // 8):
                        best = topv[0:E, 8 * r:8 * r + 8]
                        link(v.max(best, routew[0:E, :]))
                        v.max_index(topi[0:E, 8 * r:8 * r + 8], best, routew[0:E, :])
                        link(v.match_replace(routew[0:E, :], best, routew[0:E, :], -1.0))
                    link(v.tensor_copy(topf[0:E, :], topi[0:E, :]))
                    v.tensor_tensor(dgi[0:E, :].rearrange("p (e c) -> p e c", e=E), delta[0:E, :, :],
                                    bcast(topf[0:E, :], 1, E), ALU.mult)
                    for dst, src in ((top4f, topf), (top4g, topv)):
                        ins = v.tensor_copy(dst[0:E, :].rearrange("p (j c) -> p j c", j=FJ), bcast(src[0:E, :], 1, FJ))
                    sent(ins, top_ready)
                elif kind == "spread":
                    is_full(dve, job)
                    for t in range(T):
                        ins = v.tensor_scalar(pick[:, t, :], pb(job)[:, :], tok_part[:, t:t + 1], None, ALU.is_equal)
                    freed(ins, job)
                elif kind == "cols":
                    read(job, ecols_, pb(job)[:, 0:2 * E])
                    is_read(dve, job)

            with dve.Fori(0, E // 2) as it:
                for x in range(2):
                    n_ = it * 2 + (x + 1)
                    e = it * 2 + x
                    v.tensor_copy(pick_e, pick[:, :, bass.ds(e * CAP, CAP)]).then_inc(pick_e_ready, 1)
                    dve.wait_ge(gathered, n_)
                    v.tensor_copy(xs_, bank[5][:, 0:D // 4]).then_inc(xs_copied, 1)
                    dve.wait_ge(xs_turned, n_)
                    g0 = GAIN_ROWS["norm2"][0]
                    v.tensor_tensor(xsT.rearrange("p (j b) s -> p b j s", b=2),
                                    bank[4][:, 0:KD * CAP].rearrange("p (b j s) -> p b j s", b=2, j=4),
                                    bcast(gain[:, g0:g0 + KD].rearrange("p (j b) -> p b j", b=2), 3, CAP),
                                    ALU.mult).then_inc(xs_ready, 1)
                    v.tensor_scalar(spreadT_, tok_free[:, :], ecols[:, 0, bass.ds(e, 1)], ecols[:, 1, bass.ds(e, 1)],
                                    ALU.is_equal, ALU.mult).then_inc(spread_ready, 1)
                    dve.wait_ge(glu_ready, n_)
                    q = x * XCH + 7
                    dve.wait_ge(used[expert_slot(q)], it * 3 + q // SLOTS + 1)
                    v.tensor_tensor(hidx, bank[5][:, :], sgx, ALU.mult).then_inc(h_ready, 1)
                    q = x * XCH + XCH - 1
                    dve.wait_ge(used[expert_slot(q)], it * 3 + q // SLOTS + 1)
                    v.tensor_copy(eo[:, 1, :], bank[7][:, :]).then_inc(eo1_ready, 1)
            dve.wait_ge(gb2_loaded, 16)
            for t in range(T):
                dve.wait_ge(squares, NORM_ORDER.index((6, t)) + 1)
                link(v.tensor_tensor(stat[:, 48 + t:49 + t], stat[:, 56 + 2 * t:57 + 2 * t], stat[:, 57 + 2 * t:58 + 2 * t], ALU.add))
                mean_of(6, t, D)
                for h in range(2):
                    sent(v.scalar_tensor_tensor(UTf[:, t, h * NB:(h + 1) * NB], bank[2 * t + h][:, :], rcol(6, t),
                                                GB[:, h * NB:(h + 1) * NB], ALU.mult, ALU.mult), out_ready)

        @block.tensor
        def _(pe):
            mm = nc.tensor.matmul
            tr = nc.tensor.transpose

            def filled(ins, job):
                ins.then_inc(full[JOB[job] % BANKS], 1)

            def turn_tokens(st, t):
                for q in range(2):
                    j = st + (q,)
                    bank_taken(pe, j)
                    for b in range(4):
                        ins = tr(pb(j)[:, b * P:(b + 1) * P], SC[:, t, (4 * q + b) * P:(4 * q + b + 1) * P], ident[:, :])
                    filled(ins, j)

            def features_ready(st):
                for q in range(2):
                    is_read(pe, st + (q,))

            def tokens_by_columns(job, lhs, w, n, k_n, stride, off=0):
                bank_taken(pe, job)
                for k in range(k_n):
                    ins = mm(pb(job)[:, 0:n], lhs(k), w[:, k * stride + off:k * stride + off + n],
                             start=(k == 0), stop=(k == k_n - 1))
                filled(ins, job)

            ROTS = [st[1:] for st in STEPS if st[0] == "rot"]
            def split_product(j, t, h, x, w, end):
                for k in range(4 * h, 4 * h + 4):
                    kk = (k - 4 * h) * NB
                    for n, (x_, w_) in enumerate(((0, 0), (0, 1), (1, 0))):
                        ins = mm(pb(j)[:, :], x[:, x_, k, t * P:(t + 1) * P], w[:, w_, kk:kk + NB],
                                 start=(k == 0 and n == 0), stop=(end and k == KD - 1 and n == 2), skip_group_check=True)
                return ins

            last = sorted(JOB, key=JOB.get)[-BANKS:]
            w_rf = w_r[:, :, :].rearrange("p k e -> p (k e)")
            for st in STEPS:
                kind = st[0]
                job = st + (0,)
                if kind == "gains":
                    pe.wait_ge(consts_ready, 1)
                    pe.wait_ge(rows_loaded, 16 * 12)
                    filled(tr(pb(job)[:, 0:GAINS], UTf[0:GAINS, 0, 0:P], ident[0:GAINS, 0:GAINS]), job)
                    pe.wait_ge(conv_loaded, 16)
                    j, n = ("gains", 1), TAPS * CT
                    filled(tr(pb(j)[:, 0:n], UTf[0:n, 0, P:2 * P], ident[0:n, 0:n]), j)
                elif kind == "norm":
                    pe.wait_ge(xn_ready, T * st[1] + st[2] + 1)
                    turn_tokens(st, st[2])
                elif kind == "proj" and st[1] in SPLIT_IN:
                    _, c, t = st
                    for tt, h in ([(0, 0), (1, 0), (0, 1)] if t == 0 else [(1, 1)]):
                        j = ("proj", c, tt, 0)
                        if h == 0:
                            bank_taken(pe, j)
                        pe.wait_ge(ixl_ready, 2 * tt + h + 1)
                        pe.wait_ge(il_ready, 2 * c - 1 + h)
                        ins = split_product(j, tt, h, ixsplit, isplit[h], h == 1)
                        if h == 1:
                            filled(ins, j)
                        elif tt == T - 1:
                            ins.then_inc(ihalf_used, 1)
                elif kind == "proj":
                    _, c, t = st
                    w, n = slot(("w_in", c)), W_IN_CUTS[c][1]
                    features_ready(("norm", 0, t))
                    has_weights(pe, ("w_in", c))
                    tokens_by_columns(job, lambda k: UT[:, k, t * P:(t + 1) * P], w, n, KD, n)
                elif kind == "rot":
                    _, c, t = st
                    r = ROTS.index((c, t))
                    bank_taken(pe, job)
                    pe.wait_ge(rot_ready, r + 1)
                    nb = {KV4: 3, KV2: 1}.get(c, 4)
                    for b in range(nb):
                        ins = tr(pb(job)[:, b * P:(b + 1) * P], rot[:, r % 2, b * P:(b + 1) * P], ident[:, :])
                    filled(ins, job)
                elif kind == "cmph":
                    bank_taken(pe, job)
                    pe.wait_ge(blk_ready, 1)
                    has_weights(pe, ("cmp", 0))
                    has_weights(pe, ("cmp", 1))
                    for l in range(LP):
                        for kv in range(2):
                            ins = mm(pb(job)[32 * kv:32 * kv + 32, 0:CH], blk[:, kv, l, :, :].rearrange("p g i -> p (g i)"),
                                     slot(("cmp", kv))[:, l * CH:(l + 1) * CH], start=(l == 0), stop=(l == LP - 1),
                                     skip_group_check=True)
                    filled(ins, job)
                elif kind == "cmpt":
                    bank_taken(pe, job)
                    is_read(pe, ("cmph", 0))
                    for k in range(2):
                        ins = tr(pb(job)[:, k * 64:(k + 1) * 64], hidc[0:64, k * P:(k + 1) * P], ident[0:64, 0:64])
                    filled(ins, job)
                elif kind == "cmpw":
                    bank_taken(pe, job)
                    is_read(pe, ("cmpt", 0))
                    pe.wait_ge(small_loaded, 16 * 3)
                    for g in range(2):
                        for k in range(2):
                            mm(pb(job)[DH * g:DH * (g + 1), 0:16], w2[:, 0, k, :], hidcT[:, k, 16 * g:16 * g + 16],
                               start=(k == 0), stop=(k == 1))
                    for g in range(2):
                        for k in range(2):
                            ins = mm(pb(job)[0:16, DH * (1 + g):DH * (2 + g)], hidcT[:, k, 32 + 16 * g:48 + 16 * g],
                                     w2[:, 1, k, :], start=(k == 0), stop=(k == 1))
                    filled(ins, job)
                elif kind == "S":
                    u = st[1]
                    k, p, t = UNITS[u]
                    need = {"diff": [("rot", c, x, 0) for c in (DQ, DK) for x in range(T)],
                            "cmp": [("rot", NQ, x, 0) for x in range(T)] + [("cmpw", 0)],
                            "sel": [("rot", KV4, x, 0) for x in range(T)],
                            "win": [("rot", KV2, x, 0) for x in range(T)],
                            "grid": [("qk", c, p, 0) for c in range(2)]}[k]
                    for j in need:
                        is_read(pe, j)
                    tq = slice(t * P, (t + 1) * P)
                    w = key_tiles(u) * P
                    for s in range(2):
                        bank_taken(pe, ("S", u, s))
                    rows = [slice(DH * s, DH * (s + 1)) for s in range(2)]
                    for i in range(4 if k == "cmp" else 2):
                        for s in range(2):
                            j = ("S", u, s)
                            if k == "cmp":
                                ins = mm(pb(j)[:, 16 * i:16 * i + NCB], qkT[rows[s], 8 + i, tq], kcT[rows[s], 0:NCB],
                                         start=True, stop=True)
                                if i == 3:
                                    filled(ins, j)
                                continue
                            b = 2 * p + i
                            if k == "diff":
                                lq, rk = qkT[rows[s], b, tq], qkT[rows[s], 4 + b, 0:w]
                            elif k == "grid":
                                lq, rk = qkT2[rows[s], b, tq], qkT2[rows[s], 4 + b, 0:w]
                            else:
                                lq, rk = qkT[rows[s], 8 + b, tq], qkT[rows[s], 14 if k == "sel" else 15, 0:w]
                            ins = mm(pb(j)[:, S * i:S * i + w], lq, rk, start=True, stop=True)
                            if i == 1:
                                filled(ins, j)
                elif kind == "PT":
                    u = st[1]
                    k, p, t = UNITS[u]
                    sbuf = (probs1 if u < NU1 else probs2)[:, u % 2]
                    for j in range(turns(u)):
                        bank_taken(pe, st + (j,))
                    if k in ("diff", "cmp"):
                        pe.wait_ge(mixed_ready, u + 1)
                    else:
                        pe.wait_ge(exp_ready, u + 1)
                    if k == "cmp":
                        flat = sbuf.rearrange("p m k -> p (m k)")
                        for n in range(8):
                            ins = tr(pb(st + (n // 4,))[0:NCB, (n % 4) * P:(n % 4 + 1) * P], flat[:, 16 * n:16 * n + NCB],
                                     ident[:, :])
                            if n % 4 == 3:
                                filled(ins, st + (n // 4,))
                        continue
                    nk = key_tiles(u)
                    maps = 2 if k == "diff" else 4
                    for m in range(maps):
                        for kk in range(nk):
                            n = m * nk + kk
                            ins = tr(pb(st + (n // 4,))[:, (n % 4) * P:(n % 4 + 1) * P], sbuf[:, m, kk * P:(kk + 1) * P],
                                     ident[:, :])
                            if n % 4 == 3 or n == maps * nk - 1:
                                filled(ins, st + (n // 4,))
                elif kind == "PV":
                    u = st[1]
                    k, p, t = UNITS[u]
                    tb = (turned1 if u < NU1 else turned2)[:, u % 2]
                    bank_taken(pe, job)
                    for j in range(turns(u)):
                        is_read(pe, ("PT", u, j))
                    values = {"diff": [("proj", DV, x, 0) for x in range(T)], "cmp": [("cmpw", 0)],
                              "sel": [("proj", KV4, x, 0) for x in range(T)], "win": [("proj", KV2, x, 0) for x in range(T)],
                              "grid": [("v", x, 0) for x in range(T)]}[k]
                    for j in values:
                        is_read(pe, j)
                    if k == "cmp":
                        for n in range(8):
                            ins = mm(pb(job)[:, n * DH:(n + 1) * DH], tb[0:NCB, n * P:(n + 1) * P],
                                     vcs[0:NCB, DH * (n // 4):DH * (n // 4 + 1)], start=True, stop=True)
                        filled(ins, job)
                        continue
                    nk = key_tiles(u)
                    wd_ = P if k == "diff" else DH
                    for m in range(2 if k == "diff" else 4):
                        for kk in range(nk):
                            if k == "diff":
                                val = vdiff[:, kk, (2 * p + m) * P:(2 * p + m + 1) * P]
                            elif k == "grid":
                                hd = 2 * (2 * p + m % 2) + m // 2
                                val = v2[:, kk, hd * DH:(hd + 1) * DH]
                            else:
                                val = (vsel if k == "sel" else vwin)[:, kk, DH * (m // 2):DH * (m // 2 + 1)]
                            n = m * nk + kk
                            ins = mm(pb(job)[:, m * wd_:(m + 1) * wd_], tb[:, n * P:(n + 1) * P], val,
                                     start=(kk == 0), stop=(kk == nk - 1))
                    filled(ins, job)
                elif kind in ("yaT", "ybT", "oT"):
                    for t in (range(T) if kind == "yaT" else st[1:]):
                        j = ("yaT", t) if kind == "yaT" else job
                        bank_taken(pe, j)
                        if kind == "yaT":
                            pe.wait_ge(ya_ready, 1)
                        elif kind == "ybT":
                            pe.wait_ge(yb_added, 8)
                        else:
                            pe.wait_ge(on_ready, t + 1)
                        src = {"yaT": ya, "ybT": yb, "oT": o2}[kind]
                        for b in range(4):
                            ins = tr(pb(j)[:, b * P:(b + 1) * P], src[:, t, b * P:(b + 1) * P], ident[:, :])
                        filled(ins, j)
                elif kind in ("bra", "brb"):
                    _, t, h = st
                    src = yaT if kind == "bra" else ybT
                    has_weights(pe, (kind,))
                    is_read(pe, ("yaT", t) if kind == "bra" else ("ybT", t, 0))
                    tokens_by_columns(job, lambda k: src[:, k, t * P:(t + 1) * P], slot((kind,)), NB, 4, D, h * NB)
                elif kind == "mT":
                    pe.wait_ge(merged, 2 * st[1] + 2)
                    turn_tokens(st, st[1])
                elif kind in ("wo2c", "wo2"):
                    _, t, h = st
                    k0 = 4 if kind == "wo2c" else 0
                    bank_taken(pe, job)
                    has_weights(pe, ("wo2", h))
                    if kind == "wo2":
                        is_read(pe, ("oT", t, 0))
                    for k in range(k0, k0 + 4):
                        if kind == "wo2c":
                            pe.wait_ge(conv_mixed, k - 3)
                        ins = mm(pb(job)[:, :], UT[:, k, t * P:(t + 1) * P], slot(("wo2", h))[:, k * NB:(k + 1) * NB],
                                 start=(k == k0), stop=(k == k0 + 3))
                    filled(ins, job)
                elif kind == "wo":
                    _, t, h = st
                    has_weights(pe, (kind, h))
                    features_ready(("mT", t))
                    tokens_by_columns(job, lambda k: UT[:, k, t * P:(t + 1) * P], slot((kind, h)), NB, KD, NB)
                elif kind in ("gu", "gu_first"):
                    c, t = st[1:] if kind == "gu" else (0, 0)
                    if kind == "gu_first":
                        parts = [(0, 0)]
                    elif c == 0:
                        parts = [(0, 1)] if t == 0 else [(1, 0), (1, 1)]
                    else:
                        parts = [(0, 0), (1, 0), (0, 1)] if t == 0 else [(1, 1)]
                    for tt, h in parts:
                        j = ("gu", c, tt, 0)
                        if h == 0:
                            bank_taken(pe, j)
                        pe.wait_ge(ul_ready, 2 * tt + h + 1)
                        pe.wait_ge(wl_ready, 2 * c + h + 1)
                        ins = split_product(j, tt, h, usplit, wsplit[:, h, :, :], h == 1)
                        if h == 1:
                            filled(ins, j)
                        elif tt == T - 1:
                            ins.then_inc(half_used, 1)
                elif kind == "hT":
                    c = st[1]
                    bank_taken(pe, job)
                    for t in range(T):
                        is_read(pe, ("gu", c, t, 0))
                    for kk in range(2):
                        for t in range(T):
                            ins = tr(pb(job)[:, kk * S + t * P:kk * S + (t + 1) * P],
                                     hid[:, (2 * c + t) % 4, kk * P:(kk + 1) * P], ident[:, :])
                    filled(ins, job)
                elif kind == "dn":
                    if st[1] == 0:
                        for j in jobs_of(st):
                            bank_taken(pe, j)
                    parts = {9: [(0, 9), (0, 10)], 10: [(1, 9)], 11: [(1, 10)]}.get(st[1], [(t, st[1]) for t in range(T)])
                    for t, n in parts:
                        pe.wait_ge(dl_ready, n + 1)
                        for h in range(2):
                            for k in range(2):
                                w0 = k * D + h * NB
                                for m, (x, w) in enumerate(((0, 0), (0, 1), (1, 0))):
                                    ins = mm(pb(("down", t, h))[:, :], hsplit[:, n % 2, x, k, t * P:(t + 1) * P],
                                             wsplit[:, n % 2, w, w0:w0 + NB], start=(n == 0 and k == 0 and m == 0),
                                             stop=(n == 10 and k == 1 and m == 2), skip_group_check=True)
                            if n == 10:
                                filled(ins, ("down", t, h))
                    if st[1] < 9:
                        ins.then_inc(down_used, 1)
                elif kind == "cpe":
                    bank_taken(pe, job)
                    pe.wait_ge(u_ready, 1)
                    pe.wait_ge(diag_ready, TAPS)
                    for tap in range(TAPS):
                        ins = mm(pb(job)[:, 0:S], diag[:, tap, :], upad[:, CT - 1, tap:tap + S],
                                 start=(tap == 0), stop=(tap == TAPS - 1))
                    filled(ins, job)
                elif kind in ("qk", "ag"):
                    _, c, h = st
                    ch = ("w_in2", c if kind == "qk" else 3 + c)
                    for t in range(T):
                        features_ready(("norm", 2, t))
                    has_weights(pe, ch)
                    bank_taken(pe, job)
                    for i in range(2):
                        for k in range(KD):
                            ins = mm(pb(job)[:, i * S:(i + 1) * S], slot(ch)[:, k * NB + (2 * h + i) * P:k * NB + (2 * h + i + 1) * P],
                                     UT[:, k, :], start=(k == 0), stop=(k == KD - 1))
                    filled(ins, job)
                elif kind == "v":
                    t = st[1]
                    features_ready(("norm", 2, t))
                    has_weights(pe, ("w_in2", 2))
                    tokens_by_columns(job, lambda k: UT[:, k, t * P:(t + 1) * P], slot(("w_in2", 2)), NB, KD, NB)
                elif kind in ("cmean", "cvar", "crms"):
                    bank_taken(pe, job)
                    if kind == "cmean":
                        pe.wait_ge(conv_ready, TAPS * CV)
                        is_read(pe, ("cpe", 0))
                    else:
                        pe.wait_ge(csq_ready, 1 if kind == "cvar" else 2)
                    src = cz if kind == "cvar" else dw
                    for c in range(CT):
                        ins = mm(pb(job)[:, 0:S], ones[:, :], src[:, c, :], start=(c == 0), stop=(c == CT - 1))
                    filled(ins, job)
                elif kind == "logit":
                    t = st[1]
                    features_ready(("norm", 3, t))
                    tokens_by_columns(job, lambda k: UT[:, k, t * P:(t + 1) * P], w_rf, E, KD, E)
                elif kind == "affT":
                    bank_taken(pe, job)
                    for t in range(T):
                        pe.wait_ge(aff_ready, t + 1)
                        ins = tr(pb(job)[0:E, t * P:(t + 1) * P], aff[:, t, :], ident[:, :])
                    filled(ins, job)
                    for j in last[:4]:
                        is_read(pe, j)
                    for q in range(4):
                        mm(bank[q][:, :], ident[:, :], X[:, q // 2, (q % 2) * NB:(q % 2 + 1) * NB], start=True, stop=False,
                           skip_group_check=True)
                elif kind == "spread":
                    bank_taken(pe, job)
                    pe.wait_ge(top_ready, 1)
                    filled(mm(pb(job)[:, :], ones[0:E, :], dgi[0:E, :], start=True, stop=True), job)
                elif kind == "cols":
                    bank_taken(pe, job)
                    mm(pb(job)[:, 0:E], top4f[0:E, :], ident[0:E, 0:E], start=True, stop=True)
                    filled(mm(pb(job)[:, E:2 * E], top4g[0:E, :], ident[0:E, 0:E], start=True, stop=True), job)

            for j in last:
                is_read(pe, j)
            with pe.Fori(0, E // 2) as it:
                for x in range(2):
                    n = it * 2 + (x + 1)
                    e = it * 2 + x

                    def chunk(q):
                        s, o = expert_slot(x * XCH + q), (x * XCH + q) // SLOTS
                        pe.wait_ge(loaded[s], it * 48 + (16 * (BASE[s] + o + 1)))
                        return s

                    pe.wait_ge(pick_e_ready, n)
                    for t in range(T):
                        for j in range(4):
                            ins = mm(bank[5][32 * j:32 * j + 32, 0:D // 4], pick_e[:, t, :],
                                     SC[:, t, j * (D // 4):(j + 1) * (D // 4)], start=(t == 0), stop=(t == T - 1),
                                     tile_position=(0, 32 * j), skip_group_check=True)
                    ins.then_inc(gathered, 1)
                    pe.wait_ge(xs_copied, n)
                    for b in range(2):
                        ins = tr(bank[4][:, b * P:(b + 1) * P], xs_[:, b * P:(b + 1) * P], ident[:, :])
                    ins.then_inc(xs_turned, 1)
                    pe.wait_ge(xs_ready, n)
                    for q in range(8):
                        s = chunk(q)
                        w = ring[:, s, :].rearrange("p (k c j f) -> p k c j f", k=2, c=4, j=FJ)
                        for kk in range(2):
                            k = 2 * (q % 4) + kk
                            for j in range(FJ):
                                ins = mm(bank[4 + q // 4][32 * j:32 * j + 32, :], xsT[:, k, :], w[:, kk, :, j, :],
                                         start=(k == 0), stop=(k == KD - 1), tile_position=(0, 32 * j), skip_group_check=True)
                        ins.then_inc(used[s], 1)
                    pe.wait_ge(h_ready, n)
                    for c in range(4):
                        ins = tr(bank[4][:, c * P:(c + 1) * P], hidx[:, c * P:(c + 1) * P], ident[:, :])
                    ins.then_inc(turned_x, 1)
                    pe.wait_ge(hT_ready, n)
                    def down(q):
                        s = chunk(q)
                        w = ring[:, s, :].rearrange("p (c j f) -> p c j f", c=2, j=FJ)
                        for cc in range(2):
                            c = 2 * (q % 2) + cc
                            for j in range(FJ):
                                ins = mm(bank[6 + (q - 8) // 2][32 * j:32 * j + 32, :], hidxT[:, c, 32 * j:32 * j + 32],
                                         w[:, cc, j, :], start=(c == 0), stop=(c == 3), tile_position=(0, 32 * j),
                                         skip_group_check=True)
                        ins.then_inc(used[s], 1)

                    def add_up(h):
                        for t in range(T):
                            mm(bank[2 * t + h][:, :], spreadT_[:, t * P:(t + 1) * P], eo[:, h, :], start=False, stop=False,
                               skip_group_check=True).then_inc(y_done, 1)

                    down(8)
                    down(9)
                    down(10)
                    pe.wait_ge(spread_ready, n)
                    pe.wait_ge(eo0_ready, n)
                    add_up(0)
                    down(11)
                    pe.wait_ge(eo1_ready, n)
                    add_up(1)


_OUTS = [((1, S, D), "float32")]


def kernel(**inputs):
    import numpy as _np
    import concourse.bacc as _bacc
    from concourse import mybir as _mybir
    from concourse.bass_utils import run_bass_kernel_spmd as _run

    nc = _bacc.Bacc("TRN2", target_bir_lowering=False, num_devices=1)
    arrays, aps = {}, {}
    for name, value in inputs.items():
        a = _np.ascontiguousarray(value)
        arrays[f"in_{name}_dram"] = a
        aps[name] = nc.dram_tensor(f"in_{name}_dram", a.shape, _mybir.dt.from_np(a.dtype), kind="ExternalInput").ap()
    shape, dtype = _OUTS[0]
    out = nc.dram_tensor("out_0_dram", shape, _mybir.dt.from_np(_np.dtype(dtype)), kind="ExternalOutput").ap()
    two_blocks(nc, aps, out)
    r = _run(nc, [arrays], core_ids=[0])
    return r.results[0]["out_0_dram"]
```
